# Optimizing a Trainium2 kernel written in Bass

```python
import jax
import jax.numpy as jnp
from jax import lax
import numpy as np
import math
import jax, jax.numpy as jnp

D_MODEL = 1024
BATCH = 1
SEQ = 256
DEPTH = 2

N_A_LAYERS = DEPTH // 2
N_B_LAYERS = DEPTH - N_A_LAYERS
HEAD_DIM = 64
N_HEADS_A = D_MODEL // HEAD_DIM
WIDTH_A = N_HEADS_A * HEAD_DIM
DECAY_LORA = 64
ICLR_LORA = 64
N_HEADS_B = D_MODEL // HEAD_DIM
WIDTH_B = N_HEADS_B * HEAD_DIM
MOBA_BLOCK = 256
MOBA_TOPK = 3
QUERY_CHUNK = 16
ROPE_THETA = 500000.0
ROPE_DIM = HEAD_DIM // 4
RMS_EPS = 1e-6
GN_EPS = 64e-5
NEG = -1e30


def rms_norm(x, g):
    xf = x.astype(jnp.float32)
    y = xf * lax.rsqrt(jnp.mean(xf * xf, axis=-1, keepdims=True) + RMS_EPS)
    return (y * g.astype(jnp.float32)).astype(x.dtype)

def rope_tables(T):
    inv_freq = jnp.power(jnp.float32(ROPE_THETA), -jnp.arange(0, ROPE_DIM, 2, dtype=jnp.float32) / ROPE_DIM)
    ang = jnp.arange(T, dtype=jnp.float32)[:, None] * inv_freq[None, :]
    return jnp.cos(ang), jnp.sin(ang)

def partial_rope(x, cos, sin):
    half = ROPE_DIM // 2
    xr = x[..., :ROPE_DIM].astype(jnp.float32)
    x1, x2 = xr[..., :half], xr[..., half:]
    rot = jnp.concatenate([x1 * cos - x2 * sin, x2 * cos + x1 * sin], axis=-1)
    return jnp.concatenate([rot.astype(x.dtype), x[..., ROPE_DIM:]], axis=-1)

def rwkv7_time_mix(h, mu, w_in, w0, w2, a0, a2, k_k, k_a, r_k, gn_w, gn_b, w_out):
    B, T, D = h.shape
    H, N = N_HEADS_A, HEAD_DIM
    xx = jnp.pad(h, ((0, 0), (1, 0), (0, 0)))[:, :-1] - h
    widths = (WIDTH_A, DECAY_LORA, WIDTH_A, WIDTH_A, ICLR_LORA, WIDTH_A)
    outs = []
    off = 0
    for i, wd in enumerate(widths):
        outs.append((h + xx * mu[i]) @ w_in[:, off:off + wd])
        off += wd
    r, wdn, k, v, adn, gp = [o.astype(jnp.float32) for o in outs]
    w = -jax.nn.softplus(-(w0 + jnp.tanh(wdn) @ w2)) - 0.5
    decay = jnp.exp(-jnp.exp(w))
    a = jax.nn.sigmoid(a0 + adn @ a2)
    kk = (k * k_k).reshape(B, T, H, N)
    kk = kk / jnp.maximum(jnp.linalg.norm(kk, axis=-1, keepdims=True), 1e-12)
    k = k * (1.0 + (a - 1.0) * k_a)

    def heads_tm(z):
        return z.reshape(B, T, H, N).transpose(1, 0, 2, 3)

    r4, d4, k4, v4 = heads_tm(r), heads_tm(decay), heads_tm(k), heads_tm(v)
    kk4 = heads_tm(kk)
    b4 = kk4 * heads_tm(a)

    def step(S, inp):
        r_t, d_t, k_t, v_t, kk_t, b_t = inp
        sa = jnp.einsum('bhvk,bhk->bhv', S, kk_t)
        S = S * d_t[:, :, None, :] - sa[..., None] * b_t[:, :, None, :] + v_t[..., None] * k_t[:, :, None, :]
        y = jnp.einsum('bhvk,bhk->bhv', S, r_t)
        return S, y

    S0 = jnp.zeros((B, H, N, N), jnp.float32)
    _, y = lax.scan(step, S0, (r4, d4, k4, v4, kk4, b4))
    y = y.transpose(1, 0, 2, 3)
    mean = jnp.mean(y, axis=-1, keepdims=True)
    var = jnp.mean(jnp.square(y - mean), axis=-1, keepdims=True)
    y = ((y - mean) * lax.rsqrt(var + GN_EPS)).reshape(B, T, D) * gn_w + gn_b
    bonus = jnp.sum(r.reshape(B, T, H, N) * k.reshape(B, T, H, N) * r_k, axis=-1, keepdims=True) * v.reshape(B, T, H, N)
    y = (y + bonus.reshape(B, T, D)) * jax.nn.silu(gp)
    return y.astype(h.dtype) @ w_out

def shared_kv(x, norm_kv, w_kv, k_norm, cos, sin):
    B, T, D = x.shape
    kv = rms_norm(x, norm_kv) @ w_kv
    k = kv[..., :WIDTH_B].reshape(B, T, N_HEADS_B, HEAD_DIM).transpose(0, 2, 1, 3)
    v = kv[..., WIDTH_B:].reshape(B, T, N_HEADS_B, HEAD_DIM).transpose(0, 2, 1, 3)
    k = partial_rope(rms_norm(k, k_norm), cos, sin)
    nb = -(-T // MOBA_BLOCK)
    pad = nb * MOBA_BLOCK - T
    k = jnp.pad(k, ((0, 0), (0, 0), (0, pad), (0, 0)))
    v = jnp.pad(v, ((0, 0), (0, 0), (0, pad), (0, 0)))
    kb = k.reshape(B, N_HEADS_B, nb, MOBA_BLOCK, HEAD_DIM)
    vb = v.reshape(B, N_HEADS_B, nb, MOBA_BLOCK, HEAD_DIM)
    kmean = jnp.mean(kb.astype(jnp.float32), axis=3)
    return kb, vb, kmean

def moba_attention(h, w_in, q_norm, w_out, kb, vb, kmean, cos, sin):
    B, T, D = h.shape
    H, hd, C, BS = N_HEADS_B, HEAD_DIM, QUERY_CHUNK, MOBA_BLOCK
    nb = kb.shape[2]
    topk = min(MOBA_TOPK, nb)
    scale = 1.0 / float(np.sqrt(hd))
    proj = h @ w_in
    q = proj[..., :WIDTH_B].reshape(B, T, H, hd).transpose(0, 2, 1, 3)
    gate = proj[..., WIDTH_B:]
    q = partial_rope(rms_norm(q, q_norm), cos, sin)
    nc = T // C
    qch = q.reshape(B, H, nc, C, hd).transpose(2, 0, 1, 3, 4)
    bi = jnp.arange(B)[:, None, None, None]
    hi = jnp.arange(H)[None, :, None, None]

    def chunk_fn(args):
        qc, ci = args
        cb = (ci * C) // BS
        qpos = ci * C + jnp.arange(C)
        gs = jnp.einsum('bhcd,bhnd->bhcn', qc.astype(jnp.float32), kmean)
        gs = jnp.where(jnp.arange(nb) < cb, gs, NEG)
        _, idx = lax.top_k(gs, topk)
        valid = idx < cb
        ksel = kb[bi, hi, idx]
        vsel = vb[bi, hi, idx]
        s_sel = jnp.einsum('bhcd,bhcjsd->bhcjs', qc, ksel).astype(jnp.float32) * scale
        s_sel = jnp.where(valid[..., None], s_sel, NEG).reshape(B, H, C, topk * BS)
        kown = lax.dynamic_index_in_dim(kb, cb, axis=2, keepdims=False)
        vown = lax.dynamic_index_in_dim(vb, cb, axis=2, keepdims=False)
        s_own = jnp.einsum('bhcd,bhsd->bhcs', qc, kown).astype(jnp.float32) * scale
        kpos = cb * BS + jnp.arange(BS)
        s_own = jnp.where(kpos[None, :] <= qpos[:, None], s_own, NEG)
        p = jax.nn.softmax(jnp.concatenate([s_sel, s_own], axis=-1), axis=-1)
        p_sel = p[..., :topk * BS].reshape(B, H, C, topk, BS).astype(vb.dtype)
        p_own = p[..., topk * BS:].astype(vb.dtype)
        return jnp.einsum('bhcjs,bhcjsd->bhcd', p_sel, vsel) + jnp.einsum('bhcs,bhsd->bhcd', p_own, vown)

    o = lax.map(chunk_fn, (qch, jnp.arange(nc)))
    o = o.transpose(1, 0, 3, 2, 4).reshape(B, T, WIDTH_B)
    return (o * jax.nn.silu(gate)) @ w_out

def first_inputs(seed: int = 0) -> dict:
    key = jax.random.key(seed)
    ks = jax.random.split(key, 24)
    D, NA, NB_ = D_MODEL, N_A_LAYERS, N_B_LAYERS
    in_a = 4 * WIDTH_A + DECAY_LORA + ICLR_LORA
    nrm = jax.random.normal
    return {
        "x": nrm(ks[0], (BATCH, SEQ, D), jnp.float32),
        "norm_a": 1.0 + 0.02 * nrm(ks[1], (NA, D), jnp.float32),
        "mu_a": jax.random.uniform(ks[2], (NA, 6, D), jnp.float32),
        "w_in_a": nrm(ks[3], (NA, D, in_a), jnp.float32) * D ** -0.5,
        "w0_a": jax.random.uniform(ks[4], (NA, D), jnp.float32, -5.0, 0.0),
        "w2_a": nrm(ks[5], (NA, DECAY_LORA, D), jnp.float32) * 0.5 * DECAY_LORA ** -0.5,
        "a0_a": 0.1 * nrm(ks[6], (NA, D), jnp.float32),
        "a2_a": nrm(ks[7], (NA, ICLR_LORA, D), jnp.float32) * 0.5 * ICLR_LORA ** -0.5,
        "kk_a": 0.85 + 0.05 * nrm(ks[8], (NA, D), jnp.float32),
        "ka_a": 1.0 + 0.05 * nrm(ks[9], (NA, D), jnp.float32),
        "rk_a": 0.1 * nrm(ks[10], (NA, N_HEADS_A, HEAD_DIM), jnp.float32),
        "gn_w_a": 1.0 + 0.02 * nrm(ks[11], (NA, D), jnp.float32),
        "gn_b_a": 0.02 * nrm(ks[12], (NA, D), jnp.float32),
        "w_out_a": nrm(ks[13], (NA, WIDTH_A, D), jnp.float32) * WIDTH_A ** -0.5,
        "norm_kv": 1.0 + 0.02 * nrm(ks[14], (D,), jnp.float32),
        "w_kv": nrm(ks[15], (D, 2 * WIDTH_B), jnp.float32) * D ** -0.5,
        "k_norm": 1.0 + 0.02 * nrm(ks[16], (HEAD_DIM,), jnp.float32),
        "norm_b": 1.0 + 0.02 * nrm(ks[17], (NB_, D), jnp.float32),
        "w_in_b": nrm(ks[18], (NB_, D, 2 * WIDTH_B), jnp.float32) * D ** -0.5,
        "q_norm_b": 1.0 + 0.02 * nrm(ks[19], (NB_, HEAD_DIM), jnp.float32),
        "w_out_b": nrm(ks[20], (NB_, WIDTH_B, D), jnp.float32) * WIDTH_B ** -0.5,
    }

def first_block(x, norm_a, mu_a, w_in_a, w0_a, w2_a, a0_a, a2_a, kk_a, ka_a, rk_a, gn_w_a, gn_b_a, w_out_a,
              norm_kv, w_kv, k_norm, norm_b, w_in_b, q_norm_b, w_out_b):
    T = x.shape[1]
    cos, sin = rope_tables(T)
    kb = vb = kmean = None
    for layer in range(DEPTH):
        if layer < N_A_LAYERS:
            i = layer
            x = x + rwkv7_time_mix(rms_norm(x, norm_a[i]), mu_a[i], w_in_a[i], w0_a[i], w2_a[i], a0_a[i], a2_a[i],
                                   kk_a[i], ka_a[i], rk_a[i], gn_w_a[i], gn_b_a[i], w_out_a[i])
        else:
            if layer == N_A_LAYERS:
                kb, vb, kmean = shared_kv(x, norm_kv, w_kv, k_norm, cos, sin)
            j = layer - N_A_LAYERS
            x = x + moba_attention(rms_norm(x, norm_b[j]), w_in_b[j], q_norm_b[j], w_out_b[j], kb, vb, kmean, cos, sin)
    return x


DEPTH_2 = 1

N_META = 16
EPS = 1e-6
BLOCK = 128
D_RNN = D_MODEL
RG_BLOCKS = 8
RG_BS = D_RNN // RG_BLOCKS
CONV_W = 4
RG_C = 8.0
MLA_HEADS = 16
Q_LORA = 384
KV_LORA = 256
QK_NOPE = 64
QK_ROPE = 32
V_DIM = 64
ROPE_BASE = 10000.0
PEER_HEADS = 8
PEER_NKEYS = 128
PEER_EXPERTS = PEER_NKEYS * PEER_NKEYS
PEER_QDIM = 256
PEER_TOPK = 16

IN_SIZES = (D_RNN, D_RNN, Q_LORA, KV_LORA, QK_ROPE, D_MODEL, D_MODEL)
IN_SPLITS = tuple(int(s) for s in np.cumsum(IN_SIZES)[:-1])
D_IN = int(sum(IN_SIZES))


def _rmsnorm(x, g):
    xf = x.astype(jnp.float32)
    xf = xf * lax.rsqrt(jnp.mean(xf * xf, axis=-1, keepdims=True) + EPS)
    return xf.astype(x.dtype) * g

def _rope(x, pos):
    half = QK_ROPE // 2
    inv = jnp.power(ROPE_BASE, -jnp.arange(half, dtype=jnp.float32) * (2.0 / QK_ROPE))
    ang = pos[:, None] * inv[None, :]
    cos = jnp.cos(ang)[None, :, None, :].astype(x.dtype)
    sin = jnp.sin(ang)[None, :, None, :].astype(x.dtype)
    x1, x2 = x[..., :half], x[..., half:]
    return jnp.concatenate([x1 * cos - x2 * sin, x1 * sin + x2 * cos], axis=-1)

def _causal_conv(x, w, b):
    T = x.shape[1]
    xp = jnp.pad(x, ((0, 0), (CONV_W - 1, 0), (0, 0)))
    y = xp[:, 0:T] * w[0] + b
    for k in range(1, CONV_W):
        y = y + xp[:, k:k + T] * w[k]
    return y

def _lin_combine(e1, e2):
    a1, b1 = e1
    a2, b2 = e2
    return (a1 * a2, a2 * b1 + b2)

def _rg_lru(x, w_a, b_a, w_x, b_x, lam):
    B, T, _ = x.shape
    xb = x.reshape(B, T, RG_BLOCKS, RG_BS)
    r = jax.nn.sigmoid(jnp.einsum('btnc,ncd->btnd', xb, w_a).reshape(B, T, D_RNN) + b_a)
    i = jax.nn.sigmoid(jnp.einsum('btnc,ncd->btnd', xb, w_x).reshape(B, T, D_RNN) + b_x)
    log_a = RG_C * r.astype(jnp.float32) * jax.nn.log_sigmoid(lam.astype(jnp.float32))
    a = jnp.exp(log_a)
    u = jnp.sqrt(-jnp.expm1(2.0 * log_a)) * (i * x).astype(jnp.float32)
    _, h = lax.associative_scan(_lin_combine, (a, u), axis=1)
    return h.astype(x.dtype)

def _mla_attention(q_nope, q_rope, k_nope, k_rope, v):
    B, T, H, _ = q_nope.shape
    nb = T // BLOCK
    scale = (QK_NOPE + QK_ROPE) ** -0.5
    key_pos = jnp.arange(T)

    def to_blocks(t):
        return jnp.swapaxes(t.reshape((B, nb, BLOCK) + t.shape[2:]), 0, 1)

    def one_block(args):
        qn, qr, bi = args
        q_pos = bi * BLOCK + jnp.arange(BLOCK)
        s = (jnp.einsum('bqhd,bkhd->bhqk', qn, k_nope)
             + jnp.einsum('bqhd,bkd->bhqk', qr, k_rope)).astype(jnp.float32) * scale
        s = jnp.where(key_pos[None, :] <= q_pos[:, None], s, -1e30)
        p = jax.nn.softmax(s, axis=-1).astype(v.dtype)
        return jnp.einsum('bhqk,bkhd->bqhd', p, v)

    o = lax.map(one_block, (to_blocks(q_nope), to_blocks(q_rope), jnp.arange(nb)))
    return jnp.swapaxes(o, 0, 1).reshape(B, T, H * V_DIM)

def _peer(x, w_q, keys1, keys2, u, v):
    B, T, D = x.shape
    half = PEER_QDIM // 2
    xc = x.reshape(B * T // BLOCK, BLOCK, D)

    def one_chunk(xt):
        q = (xt @ w_q).reshape(BLOCK, PEER_HEADS, PEER_QDIM)
        s1 = jnp.einsum('chd,nd->chn', q[..., :half], keys1).astype(jnp.float32)
        s2 = jnp.einsum('chd,nd->chn', q[..., half:], keys2).astype(jnp.float32)
        t1, i1 = lax.top_k(s1, PEER_TOPK)
        t2, i2 = lax.top_k(s2, PEER_TOPK)
        cand = (t1[..., :, None] + t2[..., None, :]).reshape(BLOCK, PEER_HEADS, PEER_TOPK * PEER_TOPK)
        cidx = (i1[..., :, None] * PEER_NKEYS + i2[..., None, :]).reshape(BLOCK, PEER_HEADS, PEER_TOPK * PEER_TOPK)
        ts, sel = lax.top_k(cand, PEER_TOPK)
        idx = jnp.take_along_axis(cidx, sel, axis=-1)
        g = jax.nn.softmax(ts, axis=-1)
        act = jax.nn.gelu(jnp.einsum('chkd,cd->chk', u[idx], xt))
        coef = (g * act.astype(jnp.float32)).astype(xt.dtype)
        return jnp.einsum('chk,chkd->cd', coef, v[idx])

    return lax.map(one_chunk, xc).reshape(B, T, D)

def second_inputs(seed: int = 0) -> dict:
    key = jax.random.key(seed)
    ks = jax.random.split(key, 26)
    f32 = jnp.float32
    L = DEPTH_2

    def nrm(k, shape, scale):
        return jax.random.normal(k, shape, f32) * scale

    def gain(k, shape):
        return 1.0 + 0.01 * jax.random.normal(k, shape, f32)

    a_c = jax.random.uniform(ks[10], (L, D_RNN), f32, 0.9, 0.999)
    s = a_c ** (1.0 / RG_C)
    rg_lambda = jnp.log(s) - jnp.log1p(-s)
    return {
        'x': nrm(ks[0], (BATCH, SEQ, D_MODEL), 1.0),
        'meta_tokens': nrm(ks[1], (N_META, D_MODEL), 1.0),
        'norm1_g': gain(ks[2], (L, D_MODEL)),
        'w_in': nrm(ks[3], (L, D_MODEL, D_IN), D_MODEL ** -0.5),
        'conv_w': nrm(ks[4], (L, CONV_W, D_RNN), CONV_W ** -0.5),
        'conv_b': nrm(ks[5], (L, D_RNN), 0.01),
        'rg_wa': nrm(ks[6], (L, RG_BLOCKS, RG_BS, RG_BS), RG_BS ** -0.5),
        'rg_ba': nrm(ks[7], (L, D_RNN), 0.01),
        'rg_wx': nrm(ks[8], (L, RG_BLOCKS, RG_BS, RG_BS), RG_BS ** -0.5),
        'rg_bx': nrm(ks[9], (L, D_RNN), 0.01),
        'rg_lambda': rg_lambda,
        'w_rnn_out': nrm(ks[11], (L, D_RNN, D_MODEL), D_RNN ** -0.5),
        'q_norm_g': gain(ks[12], (L, Q_LORA)),
        'w_uq': nrm(ks[13], (L, Q_LORA, MLA_HEADS * (QK_NOPE + QK_ROPE)), Q_LORA ** -0.5),
        'kv_norm_g': gain(ks[14], (L, KV_LORA)),
        'w_ukv': nrm(ks[15], (L, KV_LORA, MLA_HEADS * (QK_NOPE + V_DIM)), KV_LORA ** -0.5),
        'w_attn_out': nrm(ks[16], (L, MLA_HEADS * V_DIM, D_MODEL), (MLA_HEADS * V_DIM) ** -0.5),
        'w_out': nrm(ks[17], (L, D_MODEL, D_MODEL), D_MODEL ** -0.5),
        'norm2_g': gain(ks[18], (L, D_MODEL)),
        'peer_wq': nrm(ks[19], (L, D_MODEL, PEER_HEADS * PEER_QDIM), D_MODEL ** -0.5),
        'peer_keys1': nrm(ks[20], (L, PEER_NKEYS, PEER_QDIM // 2), (PEER_QDIM // 2) ** -0.5),
        'peer_keys2': nrm(ks[21], (L, PEER_NKEYS, PEER_QDIM // 2), (PEER_QDIM // 2) ** -0.5),
        'peer_u': nrm(ks[22], (L, PEER_EXPERTS, D_MODEL), D_MODEL ** -0.5),
        'peer_v': nrm(ks[23], (L, PEER_EXPERTS, D_MODEL), PEER_HEADS ** -0.5),
        'final_g': gain(ks[24], (D_MODEL,)),
    }

def second_block(x, meta_tokens, norm1_g, w_in, conv_w, conv_b, rg_wa, rg_ba, rg_wx, rg_bx, rg_lambda,
              w_rnn_out, q_norm_g, w_uq, kv_norm_g, w_ukv, w_attn_out, w_out, norm2_g,
              peer_wq, peer_keys1, peer_keys2, peer_u, peer_v, final_g):
    B, S, D = x.shape
    T = N_META + S
    Tp = -(-T // BLOCK) * BLOCK
    meta = jnp.broadcast_to(meta_tokens[None].astype(x.dtype), (B, N_META, D))
    h = jnp.concatenate([meta, x], axis=1)
    h = jnp.pad(h, ((0, 0), (0, Tp - T), (0, 0)))
    pos = jnp.arange(Tp, dtype=jnp.float32)
    for l in range(DEPTH_2):
        n1 = _rmsnorm(h, norm1_g[l])
        xr, gr, cq, ckv, kr, g_rnn, g_att = jnp.split(n1 @ w_in[l], IN_SPLITS, axis=-1)
        hr = _rg_lru(_causal_conv(xr, conv_w[l], conv_b[l]), rg_wa[l], rg_ba[l], rg_wx[l], rg_bx[l], rg_lambda[l])
        y_rnn = (hr * jax.nn.gelu(gr)) @ w_rnn_out[l]
        q = (_rmsnorm(cq, q_norm_g[l]) @ w_uq[l]).reshape(B, Tp, MLA_HEADS, QK_NOPE + QK_ROPE)
        kv = (_rmsnorm(ckv, kv_norm_g[l]) @ w_ukv[l]).reshape(B, Tp, MLA_HEADS, QK_NOPE + V_DIM)
        q_rope = _rope(q[..., QK_NOPE:], pos)
        k_rope = _rope(kr[:, :, None, :], pos)[:, :, 0, :]
        o = _mla_attention(q[..., :QK_NOPE], q_rope, kv[..., :QK_NOPE], k_rope, kv[..., QK_NOPE:])
        y_att = o @ w_attn_out[l]
        mixed = jax.nn.sigmoid(g_rnn) * y_rnn + jax.nn.sigmoid(g_att) * y_att
        h = h + mixed @ w_out[l]
        h = h + _peer(_rmsnorm(h, norm2_g[l]), peer_wq[l], peer_keys1[l], peer_keys2[l], peer_u[l], peer_v[l])
    h = _rmsnorm(h, final_g)
    return h[:, N_META:N_META + S]


def setup_inputs(seed=0):
    out = dict(first_inputs(seed))
    for name, value in second_inputs(seed + 1).items():
        if name != "x":
            out[name + "_2"] = value
    return out


def reference(
    x, norm_a, mu_a, w_in_a, w0_a, w2_a, a0_a, a2_a, kk_a, ka_a, rk_a, gn_w_a, gn_b_a, w_out_a,
    norm_kv, w_kv, k_norm, norm_b, w_in_b, q_norm_b, w_out_b, meta_tokens_2, norm1_g_2, w_in_2,
    conv_w_2, conv_b_2, rg_wa_2, rg_ba_2, rg_wx_2, rg_bx_2, rg_lambda_2, w_rnn_out_2,
    q_norm_g_2, w_uq_2, kv_norm_g_2, w_ukv_2, w_attn_out_2, w_out_2, norm2_g_2, peer_wq_2,
    peer_keys1_2, peer_keys2_2, peer_u_2, peer_v_2, final_g_2,
):
    x = first_block(
        x, norm_a, mu_a, w_in_a, w0_a, w2_a, a0_a, a2_a, kk_a, ka_a, rk_a, gn_w_a, gn_b_a,
        w_out_a, norm_kv, w_kv, k_norm, norm_b, w_in_b, q_norm_b, w_out_b,
    )
    return second_block(
        x, meta_tokens_2, norm1_g_2, w_in_2, conv_w_2, conv_b_2, rg_wa_2, rg_ba_2, rg_wx_2,
        rg_bx_2, rg_lambda_2, w_rnn_out_2, q_norm_g_2, w_uq_2, kv_norm_g_2, w_ukv_2,
        w_attn_out_2, w_out_2, norm2_g_2, peer_wq_2, peer_keys1_2, peer_keys2_2, peer_u_2,
        peer_v_2, final_g_2,
    )


_drawn_inputs = setup_inputs


def setup_inputs(seed=0):
    import zlib

    import numpy as np

    out = dict(_drawn_inputs(seed))
    spreads = {}
    factors = {'gn_w_a': 3.192,
     'gn_b_a': 3.029,
     'norm_kv': 5.745,
     'k_norm': 6.43,
     'norm_b': 5.958,
     'q_norm_b': 8.0,
     'norm1_g_2': 15.472,
     'rg_ba_2': 64.0,
     'rg_bx_2': 64.0,
     'q_norm_g_2': 34.015,
     'kv_norm_g_2': 41.901,
     'norm2_g_2': 121.979,
     'final_g_2': 183.979,
     'conv_b_2': 8.0}
    for name, (base, spread) in spreads.items():
        noise = np.random.default_rng([zlib.crc32(name.encode()), seed]).standard_normal(out[name].shape)
        drawn = base * np.exp(spread * noise) if base else spread * noise
        out[name] = jnp.asarray(drawn.astype(out[name].dtype))
    for name, factor in factors.items():
        out[name] = (out[name] * factor).astype(out[name].dtype)
    return out
```

```python
from contextlib import ExitStack

import numpy as np

import concourse.bass as bass
from concourse import mybir

F32 = mybir.dt.float32
U32 = mybir.dt.uint32
ALU = mybir.AluOpType
ACT = mybir.ActivationFunctionType
AX = mybir.AxisListType

P = 128
D = 1024
KT = D // P
T = 256
NM = 16
S = NM + T
TT = T // P
H = 16
HD = 64
LORA = 64
RMS_EPS = 1e-6
GN_EPS = 64e-5
QL, KVL, ROPE = 384, 256, 32
QT, CT = QL // P, KVL // P
HP = 8
NK = 128
TOPK = 16
MLA_SCALE = float((64 + 32) ** -0.5)
MOBA_SCALE = float(HD ** -0.5)
NEG = -1e30
SLOT = 1024
RING = 8


def weight_slots():
    out = [("lora", 2 * KT * LORA)]
    for name in ("k", "v", "r", "g"):
        out += [((name, half, kp), SLOT) for half in range(2) for kp in range(KT // 2)]
    out += [(("out_a", m), SLOT) for m in range(KT)]
    out += [(("kb", m), SLOT) for m in range(KT)] + [(("qb", m), SLOT) for m in range(KT)]
    out += [(("vb", half, kp), SLOT) for half in range(2) for kp in range(KT // 2)]
    out += [(("gateb", m), SLOT) for m in range(KT)]
    out += [(("out_b", m), SLOT) for m in range(KT)]
    out += [(("cq", m), SLOT) for m in range(QT)] + [(("ckv", m), SLOT) for m in range(CT)]
    out += [(("kr", m), SLOT) for m in range(2)]
    out += [(("xr", m), SLOT) for m in range(KT)]
    out += [(("kn", m), CT * P) for m in range(KT)]
    out += [(("vm", half), CT * 512) for half in range(2)]
    out += [(("qn", m), QT * P) for m in range(KT)]
    out += [(("qr", m), 2 * QT * P) for m in range(H // 4)]
    out += [(("gr", m), SLOT) for m in range(KT)]
    for m in range(KT):
        out += [(("rnn", m), SLOT), (("gx", m), SLOT)]
    for m in range(KT):
        out += [(("att", m), SLOT), (("ga", m), SLOT)]
    out += [(("mix", m), SLOT) for m in range(KT)]
    out += [(("wq", m), SLOT) for m in range(2 * HP)]
    return out


CONST_WIDTHS = [
    ("ident", P), ("ones", P), ("headones", P), ("rotate", P), ("cum_in", P), ("cum_ex", P), ("carry", 2),
    ("tri", 4 * P), ("level", 7 * P), ("level_t", 7 * P), ("cos_b", T), ("sin_b", T), ("mask_b", 2 * T),
    ("cos_m", S), ("sin_m", S), ("mask_m", 2 * S), ("iota", TOPK),
]
CONST_AT, _at = {}, 0
for _name, _width in CONST_WIDTHS:
    CONST_AT[_name] = (_at, _width)
    _at += _width
CONST_N = _at

VEC_WIDTHS = [
    ("norm_a", KT), ("mu", 6 * KT), ("norm_kv", KT), ("norm_b", KT), ("k_norm", 1), ("q_norm", 1), ("norm1", KT),
    ("conv_w", 4 * KT), ("conv_b", KT), ("rg_ba", KT), ("rg_bx", KT), ("lam", KT), ("q_norm_g", QT),
    ("kv_norm_g", CT), ("norm2", KT),
]
VEC_AT, _at = {}, 0
for _name, _width in VEC_WIDTHS:
    VEC_AT[_name] = (_at, _width)
    _at += _width
VEC_N = _at
ROWS = ["kk", "ka", "rk", "gn_w", "gn_b", "final_g"]


def constants():
    c = np.zeros((P, CONST_N), np.float32)

    def put(name, a):
        at, width = CONST_AT[name]
        c[:, at:at + width] = np.asarray(a, np.float32).reshape(P, width)

    i = np.arange(P)
    put("ident", np.eye(P))
    put("ones", np.ones((P, P)))
    put("headones", (i[:, None] // HD) == (i[None, :] // HD))
    rot = np.zeros((P, P))
    for base in (0, HD):
        for d in range(8):
            rot[base + d + 8, base + d] = -1.0
            rot[base + d, base + d + 8] = 1.0
    put("rotate", rot)
    w, mid = -np.exp(-0.5), P // 2 - 1
    upto_mid = (i <= mid)[:, None].astype(float)
    put("cum_in", w * ((i[:, None] <= i[None, :]) - upto_mid))
    put("cum_ex", w * ((i[:, None] < i[None, :]) - upto_mid))
    put("carry", np.stack([w * (i > mid), w * (i <= mid)], 1))
    strict, incl = i[:, None] < i[None, :], i[:, None] <= i[None, :]
    put("tri", np.concatenate([strict, incl, strict, incl], 1))
    lev = []
    for n in range(7):
        s = 1 << n
        lev.append(((i[:, None] // (2 * s)) == (i[None, :] // (2 * s))) & (i[:, None] // s % 2 == 1) & (i[None, :] // s % 2 == 0))
    put("level", np.concatenate(lev, 1))
    put("level_t", np.concatenate([m.T for m in lev], 1))
    f = np.float32(500000.0) ** (-np.arange(0, 16, 2, dtype=np.float32) / 16)
    ang = np.arange(T, dtype=np.float32)[:, None] * f[None, :]
    cos, sin = np.ones((P, T)), np.zeros((P, T))
    for base in (0, 8, HD, HD + 8):
        cos[base:base + 8], sin[base:base + 8] = np.cos(ang).T, np.sin(ang).T
    put("cos_b", cos)
    put("sin_b", sin)
    q = i[:, None, None] + P * np.arange(2)[None, :, None]
    put("mask_b", np.where(np.arange(T)[None, None, :] <= q, 0.0, NEG))
    f = np.float32(10000.0) ** (-np.arange(16, dtype=np.float32) * np.float32(2.0 / 32))
    ang = np.arange(S, dtype=np.float32)[:, None] * f[None, :]
    row = i % ROPE
    put("cos_m", np.cos(ang).T[row % 16])
    put("sin_m", np.sin(ang).T[row % 16] * np.where(row < 16, -1.0, 1.0)[:, None])
    put("mask_m", np.where(np.arange(S)[None, None, :] <= q + NM, 0.0, NEG))
    put("iota", np.tile(np.arange(TOPK), (P, 1)))
    return c


def columns(v):
    return v.reshape(-1, P).T


def pack_weights(w):
    a, kv, wb = w["w_in_a"][0], w["w_kv"], w["w_in_b"][0]
    two, uq, ukv = w["w_in_2"][0], w["w_uq_2"][0], w["w_ukv_2"][0].reshape(KVL, H, 2 * HD)
    ak, av, aad, ag = D + LORA, 2 * D + LORA, 3 * D + LORA, 3 * D + 2 * LORA
    c_gr, c_cq = D, 2 * D
    c_kv, c_kr = c_cq + QL, c_cq + QL + KVL
    c_gx = c_kr + ROPE
    c_ga = c_gx + D

    def tiles(m):
        return m.reshape(-1, P, m.shape[1]).transpose(1, 0, 2).reshape(P, -1)

    def panel(m, n):
        return tiles(m[:, n * P:(n + 1) * P])

    def rows(m, half, kp):
        return tiles(m[kp * 2 * P:(kp + 1) * 2 * P, half * 512:(half + 1) * 512])

    uqh = uq.reshape(QL, H, 96)
    swap = np.r_[16:32, 0:16]
    uq_nope = uqh[:, :, :64].reshape(QL, D)
    uq_a = uqh[:, :, 64:].reshape(QL, H * ROPE)
    uq_b = uqh[:, :, 64:][:, :, swap].reshape(QL, H * ROPE)
    kr = two[:, c_kr:c_kr + ROPE]
    wide = {
        "k": a[:, ak:ak + D], "v": a[:, av:av + D], "r": a[:, :D], "g": a[:, ag:ag + D], "vb": kv[:, D:],
    }
    panels = {
        "out_a": w["w_out_a"][0], "kb": kv[:, :D], "qb": wb[:, :D], "gateb": wb[:, D:], "out_b": w["w_out_b"][0],
        "xr": two[:, :D], "gr": two[:, c_gr:c_gr + D], "cq": two[:, c_cq:c_kv], "ckv": two[:, c_kv:c_kr],
        "gx": two[:, c_gx:c_ga], "ga": two[:, c_ga:], "rnn": w["w_rnn_out_2"][0], "att": w["w_attn_out_2"][0],
        "mix": w["w_out_2"][0], "wq": w["peer_wq_2"][0], "qn": uq_nope, "kn": ukv[:, :, :HD].reshape(KVL, D),
    }
    ukv_v = ukv[:, :, HD:].reshape(KVL, D)
    out = []
    for key, width in weight_slots():
        if key == "lora":
            m = np.concatenate([tiles(a[:, D:D + LORA]), tiles(a[:, aad:aad + LORA])], 1)
        elif key[0] == "kr":
            m = tiles(np.tile(kr[:, swap] if key[1] else kr, (1, 4)))
        elif key[0] == "vm":
            m = tiles(ukv_v[:, key[1] * 512:(key[1] + 1) * 512])
        elif key[0] == "qr":
            m = np.concatenate([panel(uq_a, key[1]), panel(uq_b, key[1])], 1)
        elif key[0] in wide:
            m = rows(wide[key[0]], key[1], key[2])
        else:
            m = panel(panels[key[0]], key[1])
        out.append(np.ascontiguousarray(m).reshape(-1))
    return np.concatenate(out)


class Signal:

    def __init__(self, handle):
        self.handle, self.count = handle, 0

    def up(self):
        self.count += 1
        return self.handle, 1

    def dma(self):
        self.count += 16
        return self.handle, 16


class Core:

    def __init__(self, nc, ctx):
        self.nc, self.ctx = nc, ctx
        self.arena = self.sbuf("arena", 16 * 2048)
        self.ring = [self.sbuf(f"ring{i}", SLOT) for i in range(RING)]
        self.banks = [ctx.enter_context(nc.psum_tensor(f"bank{i}", [P, 512], F32)) for i in range(8)]
        self.bank_full = [Signal(self.sem(f"bank{i}_full")) for i in range(8)]
        self.bank_free = [Signal(self.sem(f"bank{i}_free")) for i in range(8)]
        self.slot_loaded = [self.sem(f"slot{i}_loaded") for i in range(RING)]
        self.weights_used = Signal(self.sem("weights_used"))
        self.chain = {e: Signal(self.sem(f"{e}_chain")) for e in ("act", "dve", "pool")}
        self.bank_at = {}
        self.next_bank = 0
        self.slots = weight_slots()
        self.slot_no = {key: n for n, (key, _) in enumerate(self.slots)}
        self.slot_freed = {}
        self.slots_issued = 0

    def sem(self, name):
        return self.ctx.enter_context(self.nc.semaphore(name))

    def counted(self, name):
        return Signal(self.sem(name))

    def sbuf(self, name, width):
        return self.ctx.enter_context(self.nc.sbuf_tensor(name, [P, width], F32))

    def claim(self, pe, key, b=None):
        if b is None:
            b = self.next_bank
            self.next_bank = (b + 1) % 8
        n = self.bank_full[b].count
        if n:
            pe.wait_ge(self.bank_free[b].handle, n)
        self.bank_at[key] = (b, n + 1)
        self.bank_full[b].count += 1
        return self.banks[b]

    def full(self, key):
        return self.bank_full[self.bank_at[key][0]].handle, 1

    def filled(self, eng, key):
        b, n = self.bank_at[key]
        eng.wait_ge(self.bank_full[b].handle, n)
        return self.banks[b]

    def free(self, key):
        return self.bank_free[self.bank_at[key][0]].handle, 1

    def copied(self, eng, key):
        b, n = self.bank_at[key]
        eng.wait_ge(self.bank_free[b].handle, n)

    def weights(self, pe, key):
        n = self.slot_no[key]
        pe.wait_ge(self.slot_loaded[n % RING], 16 * (n // RING + 1))
        return self.ring[n % RING]

    def used_by(self, key, bank_key):
        b, n = self.bank_at[bank_key]
        self.slot_freed[self.slot_no[key]] = (self.bank_full[b].handle, n)

    def used_now(self, key):
        handle, one = self.weights_used.up()
        self.slot_freed[self.slot_no[key]] = (handle, self.weights_used.count)
        return handle, one

    def load_weights(self, sp, stream, upto):
        while self.slots_issued < min(upto, len(self.slots)):
            n = self.slots_issued
            if n >= RING:
                sp.wait_ge(*self.slot_freed[n - RING])
            width = self.slots[n][1]
            at = P * sum(w for _, w in self.slots[:n])
            src = stream[at:at + P * width].rearrange("(p w) -> p w", p=P)
            sp.dma_start(self.ring[n % RING][:, 0:width], src).then_inc(self.slot_loaded[n % RING], 16)
            self.slots_issued += 1

    def link(self, eng, name, ins):
        chain = self.chain[name]
        ins.then_inc(*chain.up())
        eng.wait_ge(chain.handle, chain.count)


def tiles(ap, width):
    return ap.rearrange("p (n w) -> p n w", w=width)


def head_bcast(ap, n=H, width=HD):
    return ap.unsqueeze(2).to_broadcast([P, n, width])


def cst_of(g):
    def part(name, a=0, b=None):
        at, w = CONST_AT[name]
        return g.cst[:, at + a:at + (w if b is None else b)]
    return part


def vec_of(g):
    def column(name, n=0):
        at = VEC_AT[name][0] + n
        return g.vec[:, at:at + 1]
    return column


def time_mix(nc, core, g):
    claim, full, filled, free, copied, link = core.claim, core.full, core.filled, core.free, core.copied, core.link
    cst, vec, rows, small = cst_of(g), vec_of(g), g.rows, g.small
    unit = [core.arena[:, 2048 * i:2048 * (i + 1)] for i in range(16)]
    mix = {"w": unit[0], "a": unit[1], "k": unit[2], "v": unit[3], "r": unit[0], "g": unit[1]}
    mix = {name: tiles(ap, T) for name, ap in mix.items()}
    xx, hn = tiles(unit[4], T), tiles(unit[5], T)
    K, V, R, G, SIG, A, KK, tmp = (unit[6 + i] for i in range(8))
    squares = tiles(unit[13], T)
    lora2 = g.lora2
    E, Ei, Ep = unit[0], unit[14], unit[2]
    ar = core.arena[:, 3 * 2048:5 * 2048].rearrange("p (j a t) -> p j a t", j=KT, a=2)
    kT, bT = tiles(unit[5], T), tiles(unit[15], T)
    turned = {"a": ar[:, :, 0, :], "r": ar[:, :, 1, :], "k": kT, "b": bT, "y": kT}
    LL = [tiles(unit[n], 512) for n in (0, 1, 2, 10)]
    X, XT, TB = tiles(unit[8], P), tiles(unit[12], P), tiles(unit[13], P)
    RHS, U = unit[14][:, 0:D], unit[14][:, D:2 * D]
    y_squares = [RHS, unit[13][:, 0:D]]
    tw = {"w": unit[13][:, 0:T], "a": unit[13][:, T:2 * T]}
    x = tiles(g.res, S)[:, :, NM:]
    rstd, state = g.wide[:, 0:T], g.wide[:, T:T + 512]
    carry = small[:, 0:KT]
    key_norm, bonus, mean, inv_dev = (small[:, 32 * i:32 * i + 32] for i in range(1, 5))
    place = [(h // 2, HD * (h % 2)) for h in range(H)]
    group = [[8 * (n // 2) + n % 2 + 2 * i for i in range(4)] for n in range(4)]
    parity = [[2 * i + p for i in range(8)] for p in range(2)]
    seat = {h: 4 * n + i for n in range(4) for i, h in enumerate(group[n])}

    def by_parity(ap, h):
        at = (h % 2) * 512 + (h // 2) * HD
        return ap[:, at:at + HD]

    def tok(ap, t):
        return ap[:, t * D:(t + 1) * D]

    def sig(name):
        return core.counted("a_" + name)

    squared, rms_ready, mixed, low_ready, ones_set = sig("squared"), sig("rms"), sig("mixed"), sig("low"), sig("ones")
    gate_sigmoid, key_squares, norms, scaled = sig("gate_sigmoid"), sig("key_squares"), sig("norms"), sig("scaled")
    identity_set, xt_started, state_ready = sig("identity"), sig("xt_started"), sig("state")
    centred, y_squared, variance, deviation, y_ready = sig("centred"), sig("y_squared"), sig("variance"), sig("dev"), sig("y")
    turn_names = ("a", "r", "k", "b")

    with nc.Block() as block:
        @block.tensor
        def _(pe):
            pe.wait_ge(g.ones_loaded.handle, 16)
            bank = claim(pe, "ss_a")
            for j in range(KT):
                pe.wait_ge(squared.handle, 2 * j // KT + 1)
                mm = nc.tensor.matmul(bank[:, 0:T], cst("ones"), squares[:, j, :], start=j == 0, stop=j == KT - 1)
            mm.then_inc(*full("ss_a"))
            slot = core.weights(pe, "lora")
            for n, name in enumerate(("w", "a")):
                bank = claim(pe, ("lora", name))
                for k in range(KT):
                    pe.wait_ge(mixed.handle, n * KT + k + 1)
                    w = slot[:, (n * KT + k) * LORA:(n * KT + k + 1) * LORA]
                    mm = nc.tensor.matmul(bank[0:LORA, 0:T], w, mix[name][:, k, :], start=k == 0, stop=k == KT - 1)
                mm.then_inc(*full(("lora", name)))
            core.used_by("lora", ("lora", "a"))
            pe.wait_ge(g.lora_loaded.handle, 16)
            pe.wait_ge(ones_set.handle, 1)
            for n, name in enumerate(("w", "a")):
                copied(pe, ("lora", name))
                for t in range(TT):
                    for half in range(2):
                        key = ("z", name, t, half)
                        bank = claim(pe, key)
                        w2 = lora2[0:LORA + 1, n * D + half * 512:n * D + (half + 1) * 512]
                        nc.tensor.matmul(bank[:, :], tw[name][0:LORA + 1, t * P:(t + 1) * P], w2,
                                         start=True, stop=True).then_inc(*full(key))
            def project(n, name):
                pe.wait_ge(mixed.handle, 2 * KT + n + 1)
                for half in range(2):
                    banks = [claim(pe, (name, t, half)) for t in range(TT)]
                    for kp in range(KT // 2):
                        key = (name, half, kp)
                        slot = core.weights(pe, key)
                        for t in range(TT):
                            for i in range(2):
                                k = 2 * kp + i
                                mm = nc.tensor.matmul(banks[t][:, :], mix[name][:, k, t * P:(t + 1) * P],
                                                      slot[:, i * 512:(i + 1) * 512], start=k == 0, stop=k == KT - 1)
                            if kp == KT // 2 - 1:
                                mm.then_inc(*full((name, t, half)))
                        if kp < KT // 2 - 1:
                            mm.then_inc(*core.used_now(key))
                        else:
                            core.used_by(key, (name, TT - 1, half))
            for n, name in enumerate(("k", "v", "r")):
                project(n, name)
            pe.wait_ge(g.cst_loaded.handle, 16)
            for kind in ("cum_in", "cum_ex"):
                for t in range(TT):
                    for half in range(2):
                        key = (kind, t, half)
                        bank = claim(pe, key)
                        nc.tensor.matmul(bank[:, :], cst(kind), tok(SIG, t)[:, half * 512:(half + 1) * 512],
                                         start=True, stop=True).then_inc(*full(key))
            bank = claim(pe, "carry")
            for j in range(KT):
                for t in range(TT):
                    mm = nc.tensor.matmul(bank[:, j:j + 1], tok(SIG, t)[:, j * P:(j + 1) * P], cst("carry", t, t + 1),
                                          start=t == 0, stop=t == 1)
            mm.then_inc(*full("carry"))
            project(3, "g")
            for t in range(TT):
                for n, (name, src) in enumerate(zip(turn_names, (KK, R, K, A))):
                    pe.wait_ge(scaled.handle, 4 * t + n + 1)
                    for quad in range(2):
                        key = ("turn", name, t, quad)
                        bank = claim(pe, key)
                        for i in range(4):
                            j = 4 * quad + i
                            mm = nc.tensor.transpose(bank[:, i * P:(i + 1) * P], tok(src, t)[:, j * P:(j + 1) * P], cst("ident"))
                        mm.then_inc(*full(key))
            for quad in range(2):
                copied(pe, ("turn", "b", TT - 1, quad))
            for c in range(TT):
                at = slice(c * P, (c + 1) * P)
                for grp in range(4):
                    for h in group[grp]:
                        j, q = place[h]
                        key = ("ll", c, h)
                        bank = claim(pe, key)
                        rhs = ar[q:q + HD, j, :, at]
                        nc.tensor.matmul(bank[:, 0:T], bT[q:q + HD, j, at], rhs, start=True, stop=True)
                        nc.tensor.matmul(bank[:, T:2 * T], kT[q:q + HD, j, at], rhs, start=True, stop=True)\
                          .then_inc(*full(key))
                    key = ("lab", c, grp)
                    bank = claim(pe, key)
                    for i in range(4):
                        j, q = place[group[grp][i]]
                        mm = nc.tensor.matmul(bank[:, i * P:(i + 1) * P], ar[q:q + HD, j, 0, at], bT[q:q + HD, j, at],
                                              start=True, stop=True)
                    mm.then_inc(*full(key))
                for lev in range(1, 7):
                    for grp in range(4):
                        if lev == 1:
                            pe.wait_ge(xt_started.handle, 4 * c + grp + 1)
                        else:
                            copied(pe, ("dx", c, lev - 1, grp))
                        key = ("t", c, lev, grp)
                        bank = claim(pe, key)
                        for i in range(4):
                            mm = nc.tensor.matmul(bank[:, i * P:(i + 1) * P], LL[grp][:, i, 0:P], X[:, 4 * grp + i, :],
                                                  start=True, stop=True)
                        mm.then_inc(*full(key))
                    for grp in range(4):
                        copied(pe, ("t", c, lev, grp))
                        if lev > 1:
                            copied(pe, ("dt", c, lev - 1, grp))
                        if lev < 6:
                            key = ("dx", c, lev, grp)
                            bank = claim(pe, key)
                            for i in range(4):
                                n = 4 * grp + i
                                mm = nc.tensor.matmul(bank[:, i * P:(i + 1) * P], XT[:, n, :], TB[:, n, :], start=True, stop=True)
                            mm.then_inc(*full(key))
                        key = ("dt", c, lev, grp)
                        bank = claim(pe, key)
                        for i in range(4):
                            n = 4 * grp + i
                            mm = nc.tensor.matmul(bank[:, i * P:(i + 1) * P], TB[:, n, :], XT[:, n, :], start=True, stop=True)
                        mm.then_inc(*full(key))
                if c == 1:
                    pe.wait_ge(state_ready.handle, 1)
                for half in range(2):
                    key = ("rhs", c, half)
                    bank = claim(pe, key)
                    for i, h in enumerate(parity[half]):
                        j, q = place[h]
                        out = bank[:, i * HD:(i + 1) * HD]
                        mm = nc.tensor.matmul(out, LL[seat[h] // 4][:, seat[h] % 4, 2 * P:3 * P], tok(V, c)[:, h * HD:(h + 1) * HD],
                                              start=True, stop=c == 0)
                        if c == 1:
                            mm = nc.tensor.matmul(out, ar[q:q + HD, j, 0, at], state[q:q + HD, j * HD:(j + 1) * HD],
                                                  start=False, stop=True)
                    mm.then_inc(*full(key))
                copied(pe, ("dt", c, 6, 3))
                for half in range(2):
                    copied(pe, ("rhs", c, half))
                    key = ("u", c, half)
                    bank = claim(pe, key)
                    for i, h in enumerate(parity[half]):
                        mm = nc.tensor.matmul(bank[:, i * HD:(i + 1) * HD], XT[:, seat[h], :], by_parity(RHS, h),
                                              start=True, stop=True)
                    mm.then_inc(*full(key))
                for half in range(2):
                    copied(pe, ("u", c, half))
                    key = ("y", c, half)
                    bank = claim(pe, key)
                    for i, h in enumerate(parity[half]):
                        j, q = place[h]
                        out = bank[:, i * HD:(i + 1) * HD]
                        nc.tensor.matmul(out, LL[seat[h] // 4][:, seat[h] % 4, P:2 * P], by_parity(U, h), start=True, stop=False)
                        mm = nc.tensor.matmul(out, LL[seat[h] // 4][:, seat[h] % 4, 3 * P:4 * P], tok(V, c)[:, h * HD:(h + 1) * HD],
                                              start=False, stop=c == 0)
                        if c == 1:
                            mm = nc.tensor.matmul(out, ar[q:q + HD, j, 1, at], state[q:q + HD, j * HD:(j + 1) * HD],
                                                  start=False, stop=True)
                    mm.then_inc(*full(key))
                if c == 0:
                    bank = claim(pe, "state")
                    for h in range(H):
                        j, q = place[h]
                        out = bank[q:q + HD, j * HD:(j + 1) * HD]
                        nc.tensor.matmul(out, tok(A, 0)[:, h * HD:(h + 1) * HD], by_parity(U, h), start=True, stop=False)
                        mm = nc.tensor.matmul(out, tok(K, 0)[:, h * HD:(h + 1) * HD], tok(V, 0)[:, h * HD:(h + 1) * HD],
                                              start=False, stop=True)
                    mm.then_inc(*full("state"))
            for t in range(TT):
                pe.wait_ge(y_ready.handle, t + 1)
                for quad in range(2):
                    key = ("turn", "y", t, quad)
                    bank = claim(pe, key)
                    for i in range(4):
                        j = 4 * quad + i
                        mm = nc.tensor.transpose(bank[:, i * P:(i + 1) * P], tok(A, t)[:, j * P:(j + 1) * P], cst("ident"))
                    mm.then_inc(*full(key))
            for quad in range(2):
                copied(pe, ("turn", "y", TT - 1, quad))
            for m in range(KT):
                key = ("out_a", m)
                slot = core.weights(pe, key)
                bank = claim(pe, key)
                for k in range(KT):
                    mm = nc.tensor.matmul(bank[:, 0:T], slot[:, k * P:(k + 1) * P], kT[:, k, :], start=k == 0, stop=k == KT - 1)
                mm.then_inc(*full(key))
                core.used_by(key, key)

        @block.scalar
        def _(act):
            for n in range(2):
                at = slice(n * KT // 2, (n + 1) * KT // 2)
                act.wait_ge(g.x_loaded[n].handle, 16)
                nc.scalar.activation(squares[:, at, :], x[:, at, :], ACT.Square).then_inc(*squared.up())
            act.wait_ge(g.eps_set.handle, 1)
            bank = filled(act, "ss_a")
            nc.scalar.activation(rstd, bank[:, 0:T], ACT.Sqrt, bias=g.eps[:, 0:1], scale=1.0 / D).then_inc(*free("ss_a"))
            bank = filled(act, ("lora", "w"))
            nc.scalar.activation(tw["w"][0:LORA, :], bank[0:LORA, 0:T], ACT.Tanh).then_inc(*free(("lora", "w")))
            bank = filled(act, ("lora", "a"))
            nc.scalar.activation(tw["a"][0:LORA, :], bank[0:LORA, 0:T], ACT.Copy).then_inc(*free(("lora", "a")))
            for name, dst in (("w", SIG), ("a", A)):
                for t in range(TT):
                    for half in range(2):
                        key = ("z", name, t, half)
                        bank = filled(act, key)
                        nc.scalar.activation(tok(dst, t)[:, half * 512:(half + 1) * 512], bank[:, :], ACT.Sigmoid)\
                          .then_inc(*free(key))
            for name, dst in (("k", K), ("v", V), ("r", R)):
                for half in range(2):
                    for t in range(TT):
                        bank = filled(act, (name, t, half))
                        nc.scalar.activation(tok(dst, t)[:, half * 512:(half + 1) * 512], bank[:, :], ACT.Copy)\
                          .then_inc(*free((name, t, half)))
            act.wait_ge(key_squares.handle, 1)
            nc.scalar.activation(key_norm, key_norm, ACT.Sqrt).then_inc(*norms.up())
            for t in range(TT):
                for half in range(2):
                    at = slice(half * 512, (half + 1) * 512)
                    bank = filled(act, ("cum_in", t, half))
                    nc.scalar.activation(tok(E, t)[:, at], bank[:, :], ACT.Exp)
                    nc.scalar.activation(tok(Ei, t)[:, at], bank[:, :], ACT.Exp, scale=-1.0).then_inc(*free(("cum_in", t, half)))
            for t in range(TT):
                for half in range(2):
                    at = slice(half * 512, (half + 1) * 512)
                    bank = filled(act, ("cum_ex", t, half))
                    nc.scalar.activation(tok(Ep, t)[:, at], bank[:, :], ACT.Exp).then_inc(*free(("cum_ex", t, half)))
            bank = filled(act, "carry")
            nc.scalar.activation(carry, bank[:, 0:KT], ACT.Exp).then_inc(*free("carry"))
            for half in range(2):
                for t in range(TT):
                    bank = filled(act, ("g", t, half))
                    nc.scalar.activation(tok(G, t)[:, half * 512:(half + 1) * 512], bank[:, :], ACT.Sigmoid)\
                      .then_inc(*gate_sigmoid.up())
            for t in range(TT):
                for name in turn_names:
                    key = ("turn", name, t, 1)
                    bank = filled(act, key)
                    nc.scalar.activation(turned[name][:, 4:8, t * P:(t + 1) * P], tiles(bank[:, :], P), ACT.Copy)\
                      .then_inc(*free(key))

            def square_y(t):
                act.wait_ge(centred.handle, t + 1)
                nc.scalar.activation(y_squares[t], tok(A, t), ACT.Square).then_inc(*y_squared.up())

            def deviate(t):
                act.wait_ge(variance.handle, t + 1)
                nc.scalar.activation(inv_dev[:, 16 * t:16 * t + 16], inv_dev[:, 16 * t:16 * t + 16], ACT.Sqrt,
                                     bias=g.eps[:, 1:2], scale=1.0 / HD).then_inc(*deviation.up())

            def identity(dst):
                nc.scalar.activation(dst, cst("ident").unsqueeze(1).to_broadcast([P, H, P]), ACT.Copy).then_inc(*identity_set.up())

            for quad in range(2):
                filled(act, ("turn", "b", TT - 1, quad))
            identity(X)
            identity(XT)
            for c in range(TT):
                for lev in range(1, 7):
                    for grp in range(4):
                        key = ("t", c, lev, grp)
                        bank = filled(act, key)
                        nc.scalar.activation(TB[:, 4 * grp:4 * grp + 4, :], tiles(bank[:, :], P), ACT.Copy)\
                          .then_inc(*free(key))
                    if c == 1 and lev == 3:
                        square_y(0)
                    if c == 1 and lev == 5:
                        deviate(0)
                if c == 0:
                    filled(act, ("t", c, 6, 3))
                    identity(X)
                for name, dst in (("rhs", RHS), ("u", U)):
                    for half in range(2):
                        key = (name, c, half)
                        bank = filled(act, key)
                        nc.scalar.activation(dst[:, half * 512:(half + 1) * 512], bank[:, :], ACT.Copy).then_inc(*free(key))
                if c == 0:
                    filled(act, ("u", c, 1))
                    identity(XT)
                if c == 0:
                    filled(act, "state")
                for half in range(2):
                    key = ("y", c, half)
                    bank = filled(act, key)
                    nc.scalar.activation(tiles(tok(A, c), HD)[:, half::2, :], tiles(bank[:, :], HD), ACT.Copy).then_inc(*free(key))
            square_y(1)
            deviate(1)
            for t in range(TT):
                key = ("turn", "y", t, 1)
                bank = filled(act, key)
                nc.scalar.activation(turned["y"][:, 4:8, t * P:(t + 1) * P], tiles(bank[:, :], P), ACT.Copy)\
                  .then_inc(*free(key))
            for m in range(KT):
                copied(act, ("out_a", m))
                nc.scalar.activation(tiles(unit[15], T)[:, m, :], x[:, m, :], ACT.Square).then_inc(*g.squared_b.up())

        @block.vector
        def _(dve):
            def lk(ins):
                link(dve, "dve", ins)

            copied(dve, "ss_a")
            lk(nc.vector.reciprocal(rstd, rstd))
            dve.wait_ge(g.vec_loaded.handle, 16)
            for j in range(KT):
                ins = nc.vector.scalar_tensor_tensor(out=hn[:, j, :], in0=x[:, j, :], scalar=vec("norm_a", j), in1=rstd,
                                                     op0=ALU.mult, op1=ALU.mult)
            lk(ins)
            nc.vector.tensor_scalar(xx[:, :, 0:1], hn[:, :, 0:1], -1.0, None, ALU.mult)
            for n in range(4):
                at = slice(2 * n, 2 * n + 2)
                ins = nc.vector.tensor_tensor(xx[:, at, 1:T], hn[:, at, 0:T - 1], hn[:, at, 1:T], ALU.subtract)
                if n == 0:
                    lk(ins)
                    for j in range(2):
                        nc.vector.scalar_tensor_tensor(out=mix["w"][:, j, :], in0=xx[:, j, :], scalar=vec("mu", KT + j),
                                                       in1=hn[:, j, :], op0=ALU.mult, op1=ALU.add).then_inc(*mixed.up())
            lk(ins)
            for name, n in (("w", 1), ("a", 4), ("k", 2), ("v", 3), ("r", 0), ("g", 5)):
                if name == "r":
                    filled(dve, ("lora", "w"))
                if name == "g":
                    filled(dve, ("lora", "a"))
                for j in range(2 if name == "w" else 0, KT):
                    ins = nc.vector.scalar_tensor_tensor(out=mix[name][:, j, :], in0=xx[:, j, :], scalar=vec("mu", n * KT + j),
                                                         in1=hn[:, j, :], op0=ALU.mult, op1=ALU.add)
                    if name in ("w", "a") or j == KT - 1:
                        ins.then_inc(*mixed.up())
            dve.wait_ge(g.rows_loaded.handle, 48)
            filled(dve, ("z", "a", 1, 1))
            copied(dve, ("k", 1, 1))
            for t in range(TT):
                ins = nc.vector.tensor_tensor(tok(KK, t), tok(K, t), rows[0], ALU.mult)
            lk(ins)
            for t in range(TT):
                ins = nc.vector.tensor_tensor(tok(tmp, t), tok(KK, t), tok(KK, t), ALU.mult)
            lk(ins)
            nc.vector.tensor_reduce(key_norm, tiles(tmp, HD), AX.X, ALU.add).then_inc(*key_squares.up())
            dve.wait_ge(key_squares.handle, 1)
            copied(dve, ("z", "a", 1, 1))
            for t in range(TT):
                ins = nc.vector.scalar_tensor_tensor(out=tok(tmp, t), in0=tok(A, t), scalar=-1.0, in1=rows[1], op0=ALU.add, op1=ALU.mult)
            lk(ins)
            lk(nc.vector.scalar_tensor_tensor(out=K, in0=tmp, scalar=1.0, in1=K, op0=ALU.add, op1=ALU.mult))
            copied(dve, ("r", 1, 1))
            lk(nc.vector.tensor_tensor(tmp, R, K, ALU.mult))
            for t in range(TT):
                ins = nc.vector.tensor_tensor(tok(tmp, t), tok(tmp, t), rows[2], ALU.mult)
            lk(ins)
            lk(nc.vector.tensor_reduce(bonus, tiles(tmp, HD), AX.X, ALU.add))
            dve.wait_ge(norms.handle, 1)
            lk(nc.vector.tensor_scalar(key_norm, key_norm, 1e-12, None, ALU.max))
            lk(nc.vector.reciprocal(key_norm, key_norm))
            lk(nc.vector.tensor_tensor(tiles(KK, HD), tiles(KK, HD), head_bcast(key_norm, 2 * H), ALU.mult))
            lk(nc.vector.tensor_tensor(A, A, KK, ALU.mult))
            copied(dve, ("cum_ex", 1, 1))
            for t in range(TT):
                nc.vector.scalar_tensor_tensor(out=tok(KK, t), in0=tok(KK, t), scalar=-1.0, in1=tok(Ep, t), op0=ALU.mult,
                                               op1=ALU.mult).then_inc(*scaled.up())
                for dst, by in ((R, E), (K, Ei), (A, Ei)):
                    nc.vector.tensor_tensor(tok(dst, t), tok(dst, t), tok(by, t), ALU.mult).then_inc(*scaled.up())
            for half in range(2):
                for t in range(TT):
                    key = ("g", t, half)
                    dve.wait_ge(gate_sigmoid.handle, 2 * half + t + 1)
                    bank = filled(dve, key)
                    at = tok(G, t)[:, half * 512:(half + 1) * 512]
                    nc.vector.tensor_tensor(at, bank[:, :], at, ALU.mult).then_inc(*free(key))
            for t in range(TT):
                for name in turn_names:
                    key = ("turn", name, t, 0)
                    bank = filled(dve, key)
                    nc.vector.tensor_copy(turned[name][:, 0:4, t * P:(t + 1) * P], tiles(bank[:, :], P)).then_inc(*free(key))
            filled(dve, "carry")

            def centre(t):
                m, y = mean[:, 16 * t:16 * t + 16], tok(A, t)
                copied(dve, ("y", t, 1))
                lk(nc.vector.tensor_reduce(m, tiles(y, HD), AX.X, ALU.add))
                lk(nc.vector.tensor_scalar(m, m, 1.0 / HD, None, ALU.mult))
                nc.vector.tensor_tensor(tiles(y, HD), tiles(y, HD), head_bcast(m), ALU.subtract).then_inc(*centred.up())

            def vary(t):
                dve.wait_ge(y_squared.handle, t + 1)
                nc.vector.tensor_reduce(inv_dev[:, 16 * t:16 * t + 16], tiles(y_squares[t], HD), AX.X, ALU.add)\
                  .then_inc(*variance.up())

            def prepare(t):
                extra, gate = tok(K, t), tok(G, t)
                if t == 0:
                    filled(dve, "state")
                else:
                    copied(dve, ("turn", "b", t, 1))
                dve.wait_ge(g.rows_reloaded.handle, 32)
                lk(nc.vector.tensor_tensor(tiles(extra, HD), tiles(tok(V, t), HD), head_bcast(bonus[:, 16 * t:16 * t + 16]), ALU.mult))
                lk(nc.vector.tensor_tensor(extra, extra, rows[1], ALU.add))
                lk(nc.vector.tensor_tensor(extra, extra, gate, ALU.mult))
                lk(nc.vector.tensor_tensor(gate, gate, rows[0], ALU.mult))

            def finish_y(t):
                d, y = inv_dev[:, 16 * t:16 * t + 16], tok(A, t)
                dve.wait_ge(deviation.handle, t + 1)
                lk(nc.vector.reciprocal(d, d))
                lk(nc.vector.tensor_tensor(tiles(y, HD), tiles(y, HD), head_bcast(d), ALU.mult))
                lk(nc.vector.tensor_tensor(y, y, tok(G, t), ALU.mult))
                nc.vector.tensor_tensor(y, y, tok(K, t), ALU.add).then_inc(*y_ready.up())

            def level(name, lev):
                return cst(name, lev * P, (lev + 1) * P).bitcast(U32).unsqueeze(1).to_broadcast([P, 4, P])

            for c in range(TT):
                if c == 1:
                    filled(dve, ("y", 0, 1))
                for grp in range(4):
                    for i in range(4):
                        key = ("ll", c, group[grp][i])
                        bank = filled(dve, key)
                        nc.vector.tensor_tensor(LL[grp][:, i, :], bank[:, :], cst("tri"), ALU.mult).then_inc(*free(key))
                    copied(dve, ("ll", c, group[grp][3]))
                    at = slice(4 * grp, 4 * grp + 4)
                    bank = filled(dve, ("lab", c, grp))
                    dve.wait_ge(identity_set.handle, 2 * c + 1)
                    nc.vector.copy_predicated(X[:, at, :], level("level", 0), tiles(bank[:, :], P)).then_inc(*free(("lab", c, grp)))
                    dve.wait_ge(identity_set.handle, 2 * c + 2)
                    nc.vector.copy_predicated(XT[:, at, :], level("level_t", 0), LL[grp][:, :, 0:P]).then_inc(*xt_started.up())
                for lev in range(1, 7):
                    for grp in range(4):
                        at = slice(4 * grp, 4 * grp + 4)
                        if lev < 6:
                            key = ("dx", c, lev, grp)
                            bank = filled(dve, key)
                            nc.vector.copy_predicated(X[:, at, :], level("level", lev), tiles(bank[:, :], P)).then_inc(*free(key))
                        key = ("dt", c, lev, grp)
                        bank = filled(dve, key)
                        nc.vector.copy_predicated(XT[:, at, :], level("level_t", lev), tiles(bank[:, :], P)).then_inc(*free(key))
                    if c == 1 and lev == 2:
                        centre(0)
                    if c == 1 and lev == 4:
                        vary(0)
                    if (c, lev) in ((0, 3), (1, 1)):
                        prepare(1 - c)
                if c == 0:
                    bank = filled(dve, "state")
                    copied(dve, "carry")
                    nc.vector.tensor_tensor(tiles(state, HD), tiles(bank[:, :], HD), head_bcast(carry, KT), ALU.mult)\
                      .then_inc(*state_ready.up())
                    dve.wait_ge(state_ready.handle, 1)
                    dve.sem_inc(*free("state"))
                if c == 1:
                    finish_y(0)
            centre(1)
            vary(1)
            finish_y(1)
            for t in range(TT):
                key = ("turn", "y", t, 0)
                bank = filled(dve, key)
                nc.vector.tensor_copy(turned["y"][:, 0:4, t * P:(t + 1) * P], tiles(bank[:, :], P)).then_inc(*free(key))
            for m in range(KT):
                key = ("out_a", m)
                bank = filled(dve, key)
                nc.vector.tensor_tensor(x[:, m, :], x[:, m, :], bank[:, 0:T], ALU.add).then_inc(*free(key))

        @block.gpsimd
        def _(pool):
            nc.gpsimd.memset(g.eps[:, 0:1], RMS_EPS)
            nc.gpsimd.memset(g.eps[:, 1:2], GN_EPS).then_inc(*g.eps_set.up())
            pool.wait_ge(g.eps_set.handle, 1)
            filled(pool, "ss_a")
            nc.gpsimd.memset(unit[13][LORA:LORA + 1, 0:2 * T], 1.0).then_inc(*ones_set.up())
            pool.wait_ge(ones_set.handle, 1)
            pool.wait_ge(scaled.handle, 1)
            for n in range(2):
                pool.dma_start(rows[n], g.row(3 + n)).then_inc(*g.rows_reloaded.dma())

        @block.sync
        def _(sp):
            for n in range(2):
                at = slice(n * KT * S // 2, (n + 1) * KT * S // 2)
                sp.dma_start(g.res[:, at], g.res_in[:, at]).then_inc(*g.x_loaded[n].dma())
            first = 2 * P
            sp.dma_start(g.cst[:, 0:first], g.cst_in[:, 0:first]).then_inc(*g.ones_loaded.dma())
            sp.dma_start(g.vec, g.vec_in).then_inc(*g.vec_loaded.dma())
            core.load_weights(sp, g.stream, 1)
            sp.dma_start(lora2[0:LORA + 1, :], g.low2_in).then_inc(*g.lora_loaded.dma())
            core.load_weights(sp, g.stream, RING)
            sp.dma_start(g.cst[:, first:], g.cst_in[:, first:]).then_inc(*g.cst_loaded.dma())
            for n in range(3):
                sp.dma_start(rows[n], g.row(n)).then_inc(*g.rows_loaded.dma())
            core.load_weights(sp, g.stream, core.slot_no[("out_a", KT - 1)] + 1 + RING)


def moba(nc, core, g):
    claim, full, filled, free, copied, link = core.claim, core.full, core.filled, core.free, core.copied, core.link
    cst, vec = cst_of(g), vec_of(g)
    unit = [core.arena[:, 2048 * i:2048 * (i + 1)] for i in range(16)]
    x = tiles(g.res, S)[:, :, NM:]
    rstd = g.wide[:, 0:T]
    squares, xn = tiles(unit[15], T), {"kb": tiles(unit[0], T), "qb": tiles(unit[1], T)}
    rotated = {"kb": unit[2], "qb": unit[3]}
    V, gate = unit[4], unit[5]
    raw, sq = {"kb": unit[6], "qb": unit[7]}, {"kb": unit[8], "qb": unit[9]}
    scratch = unit[10]
    PT, SC = core.arena[:, 6 * 2048:9 * 2048], core.arena[:, 12 * 2048:15 * 2048]
    O, OT = unit[10], tiles(unit[11], T)
    row_max, den = g.small[:, 0:2 * H], g.small[:, 2 * H:4 * H]
    W3 = 3 * P

    def sig(name):
        return core.counted("b_" + name)

    normed, k_scaled, q_scaled = sig("normed"), sig("k_scaled"), sig("q_scaled")
    head_squares = {"kb": sig("k_squares"), "qb": sig("q_squares")}
    scaled = {"kb": k_scaled, "qb": q_scaled}
    rotated_up, gate_sigmoid, masked, probs, o_ready = sig("rotated"), sig("gate_sigmoid"), sig("masked"), sig("probs"), sig("o")
    gain = {"kb": "k_norm", "qb": "q_norm"}

    def pair(ap, p):
        return ap[:, p * 512:(p + 1) * 512]

    with nc.Block() as block:
        @block.tensor
        def _(pe):
            pe.wait_ge(g.squared_b.handle, KT)
            bank = claim(pe, "ss_b")
            for j in range(KT):
                mm = nc.tensor.matmul(bank[:, 0:T], cst("ones"), squares[:, j, :], start=j == 0, stop=j == KT - 1)
            mm.then_inc(*full("ss_b"))

            def project(name, src, p):
                key = (name, "pair", p)
                bank = claim(pe, key)
                for m in (2 * p, 2 * p + 1):
                    slot = core.weights(pe, (name, m))
                    for k in range(KT):
                        if m == 0 and name != "gateb":
                            pe.wait_ge(normed.handle, (KT if name == "qb" else 0) + k + 1)
                        mm = nc.tensor.matmul(bank[:, (m % 2) * T:(m % 2 + 1) * T], slot[:, k * P:(k + 1) * P], src[:, k, :],
                                              start=k == 0, stop=k == KT - 1)
                    if m % 2 == 0:
                        mm.then_inc(*core.used_now((name, m)))
                mm.then_inc(*full(key))
                core.used_by((name, 2 * p + 1), key)

            def head_sums(name, p):
                pe.wait_ge(head_squares[name].handle, p + 1)
                key = (name, "sum", p)
                bank = claim(pe, key)
                nc.tensor.matmul(bank[:, :], cst("headones"), pair(sq[name], p), start=True, stop=True).then_inc(*full(key))

            def rotate(name, p):
                pe.wait_ge(scaled[name].handle, p + 1)
                key = (name, "rot", p)
                bank = claim(pe, key)
                nc.tensor.matmul(bank[:, :], cst("rotate"), pair(raw[name], p), start=True, stop=True).then_inc(*full(key))

            for p in range(4):
                project("kb", xn["kb"], p)
            for p in range(4):
                project("qb", xn["qb"], p)
                head_sums("kb", p)
            for half in range(2):
                banks = [claim(pe, ("vb", t, half)) for t in range(TT)]
                for kp in range(KT // 2):
                    key = ("vb", half, kp)
                    slot = core.weights(pe, key)
                    for t in range(TT):
                        for i in range(2):
                            k = 2 * kp + i
                            mm = nc.tensor.matmul(banks[t][:, :], xn["kb"][:, k, t * P:(t + 1) * P],
                                                  slot[:, i * 512:(i + 1) * 512], start=k == 0, stop=k == KT - 1)
                        if kp == KT // 2 - 1:
                            mm.then_inc(*full(("vb", t, half)))
                    if kp < KT // 2 - 1:
                        mm.then_inc(*core.used_now(key))
                    else:
                        core.used_by(key, ("vb", TT - 1, half))
                for p in range(4):
                    if half == 0:
                        head_sums("qb", p)
                    else:
                        rotate("kb", p)
            for p in range(4):
                project("gateb", xn["qb"], p)
                rotate("qb", p)

            def scores(h):
                j, q = h // 2, HD * (h % 2)
                key = ("s_b", h)
                bank = claim(pe, key, h % 3)
                qT, kT = tiles(rotated["qb"], T)[q:q + HD, j, :], tiles(rotated["kb"], T)[q:q + HD, j, :]
                nc.tensor.matmul(bank[:, 0:P], qT[:, 0:P], kT[:, 0:P], start=True, stop=True)
                nc.tensor.matmul(bank[:, P:W3], qT[:, P:T], kT, start=True, stop=True).then_inc(*full(key))

            def turn(h):
                pe.wait_ge(probs.handle, h + 1)
                key = ("pt_b", h)
                bank = claim(pe, key, 3 + h % 2)
                for i in range(3):
                    mm = nc.tensor.transpose(bank[:, i * P:(i + 1) * P], SC[:, h * W3 + i * P:h * W3 + (i + 1) * P], cst("ident"))
                mm.then_inc(*full(key))

            def weigh(h):
                copied(pe, ("pt_b", h))
                key = ("o_b", h // 4)
                if h % 4 == 0:
                    claim(pe, key, 6 + h // 4 % 2)
                bank = core.banks[core.bank_at[key][0]]
                pt = PT[:, h * W3:(h + 1) * W3]
                out = [bank[:, (4 * t + h % 4) * HD:(4 * t + h % 4 + 1) * HD] for t in range(2)]
                v = [V[:, t * D + h * HD:t * D + (h + 1) * HD] for t in range(2)]
                nc.tensor.matmul(out[0], pt[:, 0:P], v[0], start=True, stop=True)
                nc.tensor.matmul(out[1], pt[:, P:2 * P], v[0], start=True, stop=False)
                mm = nc.tensor.matmul(out[1], pt[:, 2 * P:W3], v[1], start=False, stop=True)
                if h % 4 == 3:
                    mm.then_inc(*full(key))

            copied(pe, ("vb", 1, 1))
            for i in range(H + 3):
                if i < H:
                    if i % 4 == 0:
                        pe.wait_ge(rotated_up.handle, 4 + i // 4 + 1)
                    scores(i)
                if 2 <= i < H + 2:
                    turn(i - 2)
                if i >= 3:
                    weigh(i - 3)
            for t in range(TT):
                for quad in range(2):
                    key = ("turn", "o_b", t, quad)
                    pe.wait_ge(o_ready.handle, 2 * (quad + 1))
                    bank = claim(pe, key)
                    for i in range(4):
                        j = 4 * quad + i
                        mm = nc.tensor.transpose(bank[:, i * P:(i + 1) * P], O[:, t * D + j * P:t * D + (j + 1) * P], cst("ident"))
                    mm.then_inc(*full(key))
            copied(pe, ("turn", "o_b", TT - 1, 1))
            for m in range(KT):
                key = ("out_b", m)
                slot = core.weights(pe, key)
                bank = claim(pe, key)
                for k in range(KT):
                    mm = nc.tensor.matmul(bank[:, 0:T], slot[:, k * P:(k + 1) * P], OT[:, k, :], start=k == 0, stop=k == KT - 1)
                mm.then_inc(*full(key))
                core.used_by(key, key)

        @block.scalar
        def _(act):
            bank = filled(act, "ss_b")
            nc.scalar.activation(rstd, bank[:, 0:T], ACT.Sqrt, bias=g.eps[:, 0:1], scale=1.0 / D).then_inc(*free("ss_b"))

            def take(name, p):
                bank = filled(act, (name, "pair", p))
                nc.scalar.activation(pair(sq[name], p), bank[:, :], ACT.Square).then_inc(*head_squares[name].up())
                nc.scalar.activation(pair(raw[name], p), bank[:, :], ACT.Copy).then_inc(*free((name, "pair", p)))

            def root(name, p):
                bank = filled(act, (name, "sum", p))
                nc.scalar.activation(pair(sq[name], p), bank[:, :], ACT.Sqrt, bias=g.eps[:, 0:1], scale=1.0 / HD)\
                  .then_inc(*free((name, "sum", p)))

            for p in range(4):
                take("kb", p)
            for p in range(4):
                take("qb", p)
                root("kb", p)
            for half in range(2):
                for t in range(TT):
                    bank = filled(act, ("vb", t, half))
                    nc.scalar.activation(V[:, t * D + half * 512:t * D + (half + 1) * 512], bank[:, :], ACT.Copy)\
                      .then_inc(*free(("vb", t, half)))
                if half == 0:
                    for p in range(4):
                        root("qb", p)
            for p in range(4):
                bank = filled(act, ("gateb", "pair", p))
                nc.scalar.activation(pair(gate, p), bank[:, :], ACT.Sigmoid).then_inc(*gate_sigmoid.up())

            def exps(h):
                act.wait_ge(masked.handle, h + 1)
                for t in range(2):
                    at = slice(h * W3, h * W3 + P) if t == 0 else slice(h * W3 + P, (h + 1) * W3)
                    n = 2 * h + t
                    ins = nc.scalar.activation(SC[:, at], SC[:, at], ACT.Exp, bias=row_max[:, n:n + 1], scale=MOBA_SCALE,
                                               accum_out=den[:, n:n + 1])
                ins.then_inc(*probs.up())

            def keep(h):
                bank = filled(act, ("pt_b", h))
                nc.scalar.activation(PT[:, h * W3:(h + 1) * W3], bank[:, 0:W3], ACT.Copy).then_inc(*free(("pt_b", h)))

            for i in range(H + 2):
                if i < H:
                    exps(i)
                if i >= 2 and (i - 2) % 2:
                    keep(i - 2)
            for m in range(KT):
                copied(act, ("out_b", m))
                nc.scalar.activation(g.squares_c[:, m, :], tiles(g.res, S)[:, m, :], ACT.Square).then_inc(*g.squared_c.up())

        @block.vector
        def _(dve):
            def lk(ins):
                link(dve, "dve", ins)

            copied(dve, "ss_b")
            lk(nc.vector.reciprocal(rstd, rstd))
            for name, gain_of in (("kb", "norm_kv"), ("qb", "norm_b")):
                for j in range(KT):
                    ins = nc.vector.scalar_tensor_tensor(out=xn[name][:, j, :], in0=x[:, j, :], scalar=vec(gain_of, j), in1=rstd,
                                                         op0=ALU.mult, op1=ALU.mult)
                    ins.then_inc(*normed.up())

            def scale(name, p):
                copied(dve, (name, "sum", p))
                lk(nc.vector.reciprocal(pair(sq[name], p), pair(sq[name], p)))
                nc.vector.scalar_tensor_tensor(out=pair(raw[name], p), in0=pair(raw[name], p), scalar=vec(gain[name]),
                                               in1=pair(sq[name], p), op0=ALU.mult, op1=ALU.mult).then_inc(*scaled[name].up())

            def turn(name, p):
                bank = filled(dve, (name, "rot", p))
                cos, sin = (cst(n).unsqueeze(1).to_broadcast([P, 2, T]) for n in ("cos_b", "sin_b"))
                dve.wait_ge(scaled[name].handle, p + 1)
                nc.vector.tensor_tensor(tiles(pair(scratch, p), T), tiles(pair(raw[name], p), T), cos, ALU.mult)
                lk(nc.vector.tensor_tensor(tiles(pair(rotated[name], p), T), tiles(bank[:, :], T), sin, ALU.mult))
                nc.vector.tensor_tensor(pair(rotated[name], p), pair(rotated[name], p), pair(scratch, p), ALU.add)\
                  .then_inc(*rotated_up.up())
                dve.wait_ge(rotated_up.handle, rotated_up.count)
                dve.sem_inc(*free((name, "rot", p)))

            for p in range(4):
                scale("kb", p)
            for p in range(4):
                scale("qb", p)
            for p in range(4):
                turn("kb", p)
            for p in range(4):
                dve.wait_ge(gate_sigmoid.handle, p + 1)
                bank = filled(dve, ("gateb", "pair", p))
                nc.vector.tensor_tensor(pair(gate, p), bank[:, :], pair(gate, p), ALU.mult).then_inc(*free(("gateb", "pair", p)))
                turn("qb", p)

            def mask(h):
                bank = filled(dve, ("s_b", h))
                for t in range(2):
                    at = slice(0, P) if t == 0 else slice(P, W3)
                    width = P * (t + 1)
                    ins = nc.vector.tensor_tensor_reduce(
                        out=SC[:, h * W3 + at.start:h * W3 + at.stop], in0=bank[:, at], in1=cst("mask_b", t * T, t * T + width),
                        scale=1.0, scalar=-3e38, op0=ALU.add, op1=ALU.max, accum_out=row_max[:, 2 * h + t:2 * h + t + 1])
                ins.then_inc(*free(("s_b", h)))
                copied(dve, ("s_b", h))
                m = row_max[:, 2 * h:2 * h + 2]
                nc.vector.tensor_scalar(m, m, -MOBA_SCALE, None, ALU.mult).then_inc(*masked.up())

            def keep(h):
                bank = filled(dve, ("pt_b", h))
                nc.vector.tensor_copy(PT[:, h * W3:(h + 1) * W3], bank[:, 0:W3]).then_inc(*free(("pt_b", h)))

            def divide(n):
                bank = filled(dve, ("o_b", n))
                dve.wait_ge(probs.handle, 4 * n + 4)
                part = den[:, 8 * n:8 * n + 8]
                lk(nc.vector.reciprocal(part, part))
                for t in range(2):
                    ins = nc.vector.tensor_tensor(
                        tiles(O[:, t * D + 4 * n * HD:t * D + 4 * (n + 1) * HD], HD), tiles(bank[:, t * T:(t + 1) * T], HD),
                        part[:, t::2].unsqueeze(2).to_broadcast([P, 4, HD]), ALU.mult)
                ins.then_inc(*o_ready.up())
                dve.wait_ge(o_ready.handle, n + 1)
                dve.sem_inc(*free(("o_b", n)))

            for i in range(H + 4):
                if i < H:
                    mask(i)
                if 2 <= i < H + 2 and (i - 2) % 2 == 0:
                    keep(i - 2)
                if i >= 4 and (i - 4) % 4 == 3:
                    divide((i - 4) // 4)
            for t in range(TT):
                for quad in range(2):
                    key = ("turn", "o_b", t, quad)
                    bank = filled(dve, key)
                    at = tiles(gate, T)[:, 4 * quad:4 * quad + 4, t * P:(t + 1) * P]
                    nc.vector.tensor_tensor(OT[:, 4 * quad:4 * quad + 4, t * P:(t + 1) * P], tiles(bank[:, :], P), at, ALU.mult)\
                      .then_inc(*free(key))
            for m in range(KT):
                key = ("out_b", m)
                bank = filled(dve, key)
                nc.vector.tensor_tensor(x[:, m, :], x[:, m, :], bank[:, 0:T], ALU.add).then_inc(*free(key))

        @block.sync
        def _(sp):
            core.load_weights(sp, g.stream, core.slot_no[("out_b", KT - 1)] + 1 + RING)


def second_mix(nc, core, g):
    claim, full, filled, free, copied, link = core.claim, core.full, core.filled, core.free, core.copied, core.link
    cst, vec = cst_of(g), vec_of(g)
    taken = [0]

    def carve(width):
        taken[0] += width
        return core.arena[:, taken[0] - width:taken[0]]

    res = tiles(g.res, S)
    x = res[:, :, NM:]
    N1 = tiles(carve(KT * S), S)
    overlay = taken[0]
    T1, XRP, XC, AA, UU, T2 = carve(KT * S), carve(KT * (S + 4)), carve(KT * S), carve(KT * S), carve(KT * S), carve(KT * S)
    XR = tiles(XRP, S + 4)
    CQ, CKV = tiles(carve(QT * T), T), tiles(carve(CT * S), S)
    KN = tiles(carve(KT * S), S)
    VT, VM = carve(TT * D), carve(D)
    QN, QR, KR = carve(KT * T), carve(4 * T), carve(S)
    GR = carve(KT * T)
    PM = core.arena[0:NM, taken[0]:taken[0] + H * T]
    Y, RGW = carve(KT * T), carve(2 * KT * P)
    first_share = [core.arena[:, taken[0] + m * T:taken[0] + (m + 1) * T] for m in range(5)]
    CQ_flat = core.arena[:, overlay + 5 * KT * S + KT * (S + 4):][:, 0:QT * T]
    share = first_share + [CQ_flat[:, m * T:(m + 1) * T] for m in range(3)]
    SGW = [g.wide[:, n * T:(n + 1) * T] for n in range(4)]
    KEYS = (NM + P, S)
    SW = sum(KEYS)
    SC = core.arena[:, overlay:overlay + H * SW]
    PT = core.arena[:, overlay + H * SW:overlay + H * (SW + 3 * P)]
    SG = core.arena[:, overlay + KT * T:overlay + 2 * KT * T]
    ST = core.arena[:, overlay + 2 * KT * T:overlay + 3 * KT * T]
    O, OT = [g.rows[0], g.rows[1]], tiles(QN, T)
    rstd, q_dev, kv_dev = g.wide[:, 0:S], g.wide[:, S:S + T], g.wide[:, S + T:2 * S + T]
    row_max, den = g.small[:, 0:2 * H], g.small[:, 2 * H:4 * H]
    decay, lam_t = g.small[:, 64:72], [g.small[:, 72 + 8 * n:80 + 8 * n] for n in range(5)]
    lam = g.vec[:, VEC_AT["lam"][0]:VEC_AT["lam"][0] + KT]

    def sig(name):
        return core.counted("c_" + name)

    normed, rgw_loaded, lam_exp, lam_in, decay_ready = (
        sig(n) for n in ("normed", "rgw_loaded", "lam_exp", "lam_in", "decay"))
    q_squared, kv_squared, q_normed, kv_normed = sig("q_squared"), sig("kv_squared"), sig("q_normed"), sig("kv_normed")
    padded, convolved, gated, log_decay, tanh_done, one_less, roots, rnn_ready = (
        sig(n) for n in ("padded", "convolved", "gated", "log_decay", "tanh", "one_less", "roots", "rnn"))
    kr_ready, qr_ready, masked, probs, o_ready = sig("kr"), sig("qr"), sig("masked"), sig("probs"), sig("o")
    gate_sigmoid, mixed_ready = sig("gate_sigmoid"), sig("mixed")

    with nc.Block() as block:
        @block.tensor
        def _(pe):
            pe.wait_ge(g.squared_c.handle, KT)
            bank = claim(pe, "ss_c")
            for j in range(KT):
                mm = nc.tensor.matmul(bank[:, 0:S], cst("ones"), g.squares_c[:, j, :], start=j == 0, stop=j == KT - 1)
            mm.then_inc(*full("ss_c"))

            def panel(name, m, src, kt, width, first=0, bank=None, last=True, cols=P, at=0):
                if bank is None:
                    bank = claim(pe, (name, m))
                slot = core.weights(pe, (name, m))
                for k in range(kt):
                    if (name, m) == ("cq", 0):
                        pe.wait_ge(normed.handle, k + 1)
                    mm = nc.tensor.matmul(bank[:, first:first + width], slot[:, at + k * cols:at + (k + 1) * cols], src[:, k, :],
                                          start=k == 0, stop=k == kt - 1)
                return mm

            tokens = N1[:, :, NM:]
            for m in range(QT):
                panel("cq", m, tokens, KT, T).then_inc(*full(("cq", m)))
                core.used_by(("cq", m), ("cq", m))
            for m in range(CT):
                panel("ckv", m, N1, KT, S).then_inc(*full(("ckv", m)))
                core.used_by(("ckv", m), ("ckv", m))
            for m in range(2):
                panel("kr", m, N1, KT, S).then_inc(*full(("kr", m)))
                core.used_by(("kr", m), ("kr", m))
            pe.wait_ge(q_squared.handle, 1)
            bank = claim(pe, "ss_q")
            for j in range(QT):
                mm = nc.tensor.matmul(bank[:, 0:T], cst("ones"), tiles(T1[:, 0:QT * T], T)[:, j, :], start=j == 0, stop=j == QT - 1)
            mm.then_inc(*full("ss_q"))
            pe.wait_ge(kv_squared.handle, 1)
            bank = claim(pe, "ss_kv")
            for j in range(CT):
                mm = nc.tensor.matmul(bank[:, 0:S], cst("ones"), tiles(T2[:, 0:CT * S], S)[:, j, :], start=j == 0, stop=j == CT - 1)
            mm.then_inc(*full("ss_kv"))
            for m in range(KT):
                panel("xr", m, N1, KT, S).then_inc(*full(("xr", m)))
                core.used_by(("xr", m), ("xr", m))
            pe.wait_ge(kv_normed.handle, 1)
            for m in range(KT):
                panel("kn", m, CKV, CT, S).then_inc(*full(("kn", m)))
                core.used_by(("kn", m), ("kn", m))
            parts = ((0, NM), (NM, P), (NM + P, P))
            for half in range(2):
                slot = core.weights(pe, ("vm", half))
                for n, (at, count) in enumerate(parts):
                    key = ("vm", n, half)
                    bank = claim(pe, key)
                    for k in range(CT):
                        mm = nc.tensor.matmul(bank[0:count, :], CKV[:, k, at:at + count], slot[:, k * 512:(k + 1) * 512],
                                              start=k == 0, stop=k == CT - 1)
                    mm.then_inc(*full(key))
                core.used_by(("vm", half), ("vm", 2, half))
            pe.wait_ge(rgw_loaded.handle, 16)
            for m in range(KT):
                pe.wait_ge(convolved.handle, m // 4 + 1)
                for n in range(2):
                    key = ("rg", n, m)
                    bank = claim(pe, key)
                    w = RGW[:, (n * KT + m) * P:(n * KT + m + 1) * P]
                    nc.tensor.matmul(bank[:, 0:S], w, tiles(XC, S)[:, m, :], start=True, stop=True).then_inc(*full(key))
            pe.wait_ge(q_normed.handle, 1)
            for m in range(KT):
                panel("qn", m, CQ, QT, T).then_inc(*full(("qn", m)))
                core.used_by(("qn", m), ("qn", m))
            for m in range(H // 4):
                bank = claim(pe, ("qr", m))
                panel("qr", m, CQ, QT, T, bank=bank)
                panel("qr", m, CQ, QT, T, first=T, bank=bank, at=QT * P).then_inc(*full(("qr", m)))
                core.used_by(("qr", m), ("qr", m))
            for m in range(KT):
                panel("gr", m, tokens, KT, T).then_inc(*full(("gr", m)))
                core.used_by(("gr", m), ("gr", m))

            def scores(h):
                j, q, r = h // 2, HD * (h % 2), ROPE * (h % 4)
                key = ("s_c", h)
                bank = claim(pe, key, h % 2)
                at = 0
                for t in range(TT):
                    out, keys = bank[:, at:at + KEYS[t]], KEYS[t]
                    at += keys
                    nc.tensor.matmul(out, tiles(QN, T)[q:q + HD, j, t * P:(t + 1) * P], KN[q:q + HD, j, 0:keys],
                                     start=True, stop=False)
                    mm = nc.tensor.matmul(out, tiles(QR, T)[r:r + ROPE, h // 4, t * P:(t + 1) * P], KR[r:r + ROPE, 0:keys],
                                          start=False, stop=True)
                mm.then_inc(*full(key))

            def turn(h):
                pe.wait_ge(probs.handle, h + 1)
                p = SC[:, h * SW:(h + 1) * SW]
                key = ("pt_c", h)
                bank = claim(pe, key, 3 + h % 2)
                for i, at in enumerate((NM, KEYS[0] + NM, KEYS[0] + NM + P)):
                    mm = nc.tensor.transpose(bank[:, i * P:(i + 1) * P], p[:, at:at + P], cst("ident"))
                mm.then_inc(*full(key))
                key = ("pm_c", h // 2)
                if h % 2 == 0:
                    claim(pe, key, 5)
                bank = core.banks[core.bank_at[key][0]]
                for t, at in enumerate((0, KEYS[0])):
                    mm = nc.tensor.transpose(bank[0:NM, (h % 2) * T + t * P:(h % 2) * T + (t + 1) * P], p[:, at:at + NM], cst("ident"))
                if h % 2:
                    mm.then_inc(*full(key))

            def weigh(h):
                copied(pe, ("pt_c", h))
                copied(pe, ("pm_c", h // 2))
                key = ("o_c", h // 4)
                if h % 4 == 0:
                    claim(pe, key, 6 + h // 4 % 2)
                bank = core.banks[core.bank_at[key][0]]
                pt, pm = PT[:, h * 3 * P:(h + 1) * 3 * P], PM[:, h * T:(h + 1) * T]
                out = [bank[:, (4 * t + h % 4) * HD:(4 * t + h % 4 + 1) * HD] for t in range(2)]
                v = [VT[:, t * D + h * HD:t * D + (h + 1) * HD] for t in range(2)]
                vm = VM[0:NM, h * HD:(h + 1) * HD]
                nc.tensor.matmul(out[0], pm[:, 0:P], vm, start=True, stop=False)
                nc.tensor.matmul(out[0], pt[:, 0:P], v[0], start=False, stop=True)
                nc.tensor.matmul(out[1], pm[:, P:T], vm, start=True, stop=False)
                nc.tensor.matmul(out[1], pt[:, P:2 * P], v[0], start=False, stop=False)
                mm = nc.tensor.matmul(out[1], pt[:, 2 * P:3 * P], v[1], start=False, stop=True)
                if h % 4 == 3:
                    mm.then_inc(*full(key))

            copied(pe, ("vm", 2, 1))
            copied(pe, ("kn", KT - 1))
            copied(pe, ("qn", KT - 1))
            pe.wait_ge(kr_ready.handle, 1)
            pe.wait_ge(qr_ready.handle, 4)
            for i in range(H + 4):
                if i < H:
                    scores(i)
                if 2 <= i < H + 2:
                    turn(i - 2)
                if i >= 4:
                    weigh(i - 4)
                    m = (i - 4) // 2
                    key = ("rnn", m)
                    if i % 2 == 0:
                        pe.wait_ge(rnn_ready.handle, 1)
                        panel("rnn", m, tiles(GR, T), KT, T, bank=claim(pe, key, 2)).then_inc(*core.used_now(key))
                    else:
                        panel("gx", m, tokens, KT, T, first=T, bank=core.banks[2]).then_inc(*full(key))
                        core.used_by(("gx", m), key)
            for quad in range(2):
                for t in range(TT):
                    key = ("turn", "o_c", t, quad)
                    pe.wait_ge(o_ready.handle, 2 * (quad + 1))
                    bank = claim(pe, key)
                    for i in range(4):
                        j = 4 * quad + i
                        mm = nc.tensor.transpose(bank[:, i * P:(i + 1) * P], O[t][:, j * P:(j + 1) * P], cst("ident"))
                    mm.then_inc(*full(key))
            copied(pe, ("turn", "o_c", TT - 1, 1))
            for m in range(KT):
                key = ("att", m)
                bank = claim(pe, key)
                panel("att", m, OT, KT, T, bank=bank).then_inc(*core.used_now(key))
                panel("ga", m, tokens, KT, T, first=T, bank=bank).then_inc(*full(key))
                core.used_by(("ga", m), key)
            pe.wait_ge(mixed_ready.handle, KT)
            for m in range(KT):
                panel("mix", m, tiles(Y, T), KT, T).then_inc(*full(("mix", m)))
                core.used_by(("mix", m), ("mix", m))

        @block.scalar
        def _(act):
            bank = filled(act, "ss_c")
            nc.scalar.activation(rstd, bank[:, 0:S], ACT.Sqrt, bias=g.eps[:, 0:1], scale=1.0 / D).then_inc(*free("ss_c"))
            for m in range(QT):
                bank = filled(act, ("cq", m))
                ins = nc.scalar.activation(T1[:, m * T:(m + 1) * T], bank[:, 0:T], ACT.Square)
                if m == QT - 1:
                    ins.then_inc(*q_squared.up())
                nc.scalar.activation(CQ[:, m, :], bank[:, 0:T], ACT.Copy).then_inc(*free(("cq", m)))
            for m in range(CT):
                bank = filled(act, ("ckv", m))
                ins = nc.scalar.activation(T2[:, m * S:(m + 1) * S], bank[:, 0:S], ACT.Square)
                if m == CT - 1:
                    ins.then_inc(*kv_squared.up())
                nc.scalar.activation(CKV[:, m, :], bank[:, 0:S], ACT.Copy).then_inc(*free(("ckv", m)))
            bank = filled(act, "ss_q")
            nc.scalar.activation(q_dev, bank[:, 0:T], ACT.Sqrt, bias=g.eps[:, 0:1], scale=1.0 / QL).then_inc(*free("ss_q"))
            bank = filled(act, "ss_kv")
            nc.scalar.activation(kv_dev, bank[:, 0:S], ACT.Sqrt, bias=g.eps[:, 0:1], scale=1.0 / KVL).then_inc(*free("ss_kv"))
            for m in range(KT):
                bank = filled(act, ("xr", m))
                nc.scalar.activation(XR[:, m, 3:3 + S], bank[:, 0:S], ACT.Copy).then_inc(*free(("xr", m)))
            for m in range(KT):
                bank = filled(act, ("kn", m))
                nc.scalar.activation(KN[:, m, :], bank[:, 0:S], ACT.Copy).then_inc(*free(("kn", m)))
            for half in range(2):
                at = slice(half * 512, (half + 1) * 512)
                for n in range(3):
                    bank = filled(act, ("vm", n, half))
                    dst, src = (VM[0:NM, at], bank[0:NM, :]) if n == 0 else (VT[:, (n - 1) * D:n * D][:, at], bank[:, :])
                    nc.scalar.activation(dst, src, ACT.Copy).then_inc(*free(("vm", n, half)))
            act.wait_ge(lam_in.handle, 1)
            nc.scalar.activation(lam_t[0], lam_t[0], ACT.Exp, scale=-1.0).then_inc(*lam_exp.up())
            for m in range(KT):
                for n, (dst, bias) in enumerate(((AA, "rg_ba"), (UU, "rg_bx"))):
                    bank = filled(act, ("rg", n, m))
                    nc.scalar.activation(tiles(dst, S)[:, m, :], bank[:, 0:S], ACT.Sigmoid, bias=vec(bias, m)).then_inc(*free(("rg", n, m)))
            act.wait_ge(log_decay.handle, 1)
            nc.scalar.activation(T1, AA, ACT.Tanh)
            nc.scalar.activation(T2, AA, ACT.Exp).then_inc(*tanh_done.up())
            for m in range(KT):
                bank = filled(act, ("qn", m))
                nc.scalar.activation(tiles(QN, T)[:, m, :], bank[:, 0:T], ACT.Copy).then_inc(*free(("qn", m)))
            act.wait_ge(one_less.handle, 1)
            nc.scalar.activation(AA, AA, ACT.Sqrt, scale=-1.0).then_inc(*roots.up())
            for m in range(KT):
                bank = filled(act, ("gr", m))
                nc.scalar.activation(tiles(GR, T)[:, m, :], bank[:, 0:T], ACT.Gelu_apprx_tanh).then_inc(*free(("gr", m)))

            def exps(h):
                act.wait_ge(masked.handle, h + 1)
                at = h * SW
                for t in range(TT):
                    n = 2 * h + t
                    ins = nc.scalar.activation(SC[:, at:at + KEYS[t]], SC[:, at:at + KEYS[t]], ACT.Exp, bias=row_max[:, n:n + 1],
                                               scale=MLA_SCALE, accum_out=den[:, n:n + 1])
                    at += KEYS[t]
                ins.then_inc(*probs.up())

            def keep(h):
                bank = filled(act, ("pt_c", h))
                nc.scalar.activation(PT[:, h * 3 * P:(h + 1) * 3 * P], bank[:, 0:3 * P], ACT.Copy).then_inc(*free(("pt_c", h)))
                if h % 2:
                    bank = filled(act, ("pm_c", h // 2))
                    nc.scalar.activation(PM[:, (h - 1) * T:(h + 1) * T], bank[0:NM, :], ACT.Copy).then_inc(*free(("pm_c", h // 2)))

            for i in range(H + 5):
                if 3 <= i < H + 3:
                    keep(i - 3)
                if i >= 6 and i % 2 == 0:
                    m = (i - 6) // 2
                    bank = filled(act, ("rnn", m))
                    if m >= 4:
                        copied(act, ("rnn", m - 4))
                    nc.scalar.activation(SGW[m % 4], bank[:, T:2 * T], ACT.Sigmoid).then_inc(*gate_sigmoid.up())
                if i < H:
                    exps(i)
            for m in range(KT):
                bank = filled(act, ("att", m))
                nc.scalar.activation(SG[:, m * T:(m + 1) * T], bank[:, T:2 * T], ACT.Sigmoid).then_inc(*gate_sigmoid.up())
            for m in range(KT):
                copied(act, ("mix", m))
                nc.scalar.activation(g.squares_d[:, m, :], x[:, m, :], ACT.Square).then_inc(*g.squared_d.up())

        @block.vector
        def _(dve):
            def lk(ins):
                link(dve, "dve", ins)

            copied(dve, "ss_c")
            lk(nc.vector.reciprocal(rstd, rstd))
            for j in range(KT):
                ins = nc.vector.scalar_tensor_tensor(out=N1[:, j, :], in0=res[:, j, :], scalar=vec("norm1", j), in1=rstd,
                                                     op0=ALU.mult, op1=ALU.mult)
                ins.then_inc(*normed.up())
            lk(nc.vector.tensor_scalar(lam_t[1], lam, -1.0, None, ALU.mult))
            nc.vector.tensor_tensor(lam_t[0], lam, lam_t[1], ALU.max).then_inc(*lam_in.up())
            banks = [filled(dve, ("kr", m)) for m in range(2)]
            lk(nc.vector.tensor_tensor(AA[:, 0:S], banks[1][:, 0:S], cst("sin_m"), ALU.mult))
            dve.sem_inc(*free(("kr", 1)))
            nc.vector.tensor_tensor(KR, banks[0][:, 0:S], cst("cos_m"), ALU.mult).then_inc(*free(("kr", 0)))
            copied(dve, ("kr", 0))
            nc.vector.tensor_tensor(KR, KR, AA[:, 0:S], ALU.add).then_inc(*kr_ready.up())
            dve.wait_ge(kr_ready.handle, 1)
            lk(nc.vector.memset(XR[:, :, 0:3], 0.0))
            copied(dve, "ss_q")
            lk(nc.vector.reciprocal(q_dev, q_dev))
            for j in range(QT):
                ins = nc.vector.scalar_tensor_tensor(out=CQ[:, j, :], in0=CQ[:, j, :], scalar=vec("q_norm_g", j), in1=q_dev,
                                                     op0=ALU.mult, op1=ALU.mult)
            ins.then_inc(*q_normed.up())
            copied(dve, "ss_kv")
            lk(nc.vector.reciprocal(kv_dev, kv_dev))
            for j in range(CT):
                ins = nc.vector.scalar_tensor_tensor(out=CKV[:, j, :], in0=CKV[:, j, :], scalar=vec("kv_norm_g", j), in1=kv_dev,
                                                     op0=ALU.mult, op1=ALU.mult)
            ins.then_inc(*kv_normed.up())
            xc = tiles(XC, S)
            for part in range(2):
                copied(dve, ("xr", 4 * part + 3))
                for k in range(4):
                    for j in range(4 * part, 4 * part + 4):
                        w, src = vec("conv_w", k * KT + j), XR[:, j, k:k + S]
                        if k == 0:
                            ins = nc.vector.tensor_scalar(xc[:, j, :], src, w, vec("conv_b", j), ALU.mult, ALU.add)
                        else:
                            ins = nc.vector.scalar_tensor_tensor(out=xc[:, j, :], in0=src, scalar=w, in1=xc[:, j, :],
                                                                 op0=ALU.mult, op1=ALU.add)
                    if k < 3:
                        lk(ins)
                ins.then_inc(*convolved.up())
            dve.wait_ge(lam_exp.handle, 1)
            z, num, frac, sq, acc = lam_t
            lk(nc.vector.tensor_scalar(num, z, 2.0, None, ALU.add))
            lk(nc.vector.reciprocal(num, num))
            lk(nc.vector.tensor_tensor(frac, z, num, ALU.mult))
            lk(nc.vector.tensor_tensor(sq, frac, frac, ALU.mult))
            lk(nc.vector.tensor_scalar(acc, sq, 1.0 / 17, 1.0 / 15, ALU.mult, ALU.add))
            for n in (13, 11, 9, 7, 5, 3, 1):
                lk(nc.vector.tensor_tensor(acc, acc, sq, ALU.mult))
                lk(nc.vector.tensor_scalar(acc, acc, 1.0 / n, None, ALU.add))
            lk(nc.vector.tensor_tensor(acc, acc, frac, ALU.mult))
            lk(nc.vector.tensor_scalar(acc, acc, -16.0, None, ALU.mult))
            lk(nc.vector.tensor_scalar(z, lam, 0.0, 8.0, ALU.min, ALU.mult))
            lk(nc.vector.tensor_tensor(decay, z, acc, ALU.add))
            copied(dve, ("rg", 0, KT - 1))
            aa = tiles(AA, S)
            for j in range(KT):
                ins = nc.vector.tensor_scalar(aa[:, j, :], aa[:, j, :], decay[:, j:j + 1], None, ALU.mult)
            ins.then_inc(*log_decay.up())
            copied(dve, ("rg", 1, KT - 1))
            lk(nc.vector.tensor_tensor(UU, UU, XC, ALU.mult))
            dve.wait_ge(tanh_done.handle, 1)
            A2 = XRP[:, 0:KT * S]
            lk(nc.vector.tensor_tensor(A2, T2, T2, ALU.mult))
            nc.vector.scalar_tensor_tensor(out=AA, in0=A2, scalar=1.0, in1=T1, op0=ALU.add, op1=ALU.mult).then_inc(*one_less.up())
            dve.wait_ge(one_less.handle, 1)
            for m in range(H // 4):
                bank = filled(dve, ("qr", m))
                q, tmp = tiles(QR, T)[:, m, :], T1[:, m * T:(m + 1) * T]
                nc.vector.tensor_tensor(tmp, bank[:, T:2 * T], cst("sin_m", NM), ALU.mult)
                nc.vector.tensor_tensor(q, bank[:, 0:T], cst("cos_m", NM), ALU.mult).then_inc(*free(("qr", m)))
                copied(dve, ("qr", m))
                nc.vector.tensor_tensor(q, q, tmp, ALU.add).then_inc(*qr_ready.up())
            dve.wait_ge(roots.handle, 1)
            lk(nc.vector.tensor_tensor(UU, UU, AA, ALU.mult))
            for j in range(KT):
                ins = nc.vector.tensor_tensor_scan(xc[:, j, :], tiles(T2, S)[:, j, :], tiles(UU, S)[:, j, :], 0.0, ALU.mult, ALU.add)
            lk(ins)
            copied(dve, ("gr", KT - 1))
            gr = tiles(GR, T)
            nc.vector.tensor_tensor(gr, gr, xc[:, :, NM:], ALU.mult).then_inc(*rnn_ready.up())
            dve.wait_ge(rnn_ready.handle, 1)

            def mask(h):
                bank = filled(dve, ("s_c", h))
                at = 0
                for t in range(TT):
                    ins = nc.vector.tensor_tensor_reduce(
                        out=SC[:, h * SW + at:h * SW + at + KEYS[t]], in0=bank[:, at:at + KEYS[t]],
                        in1=cst("mask_m", t * S, t * S + KEYS[t]), scale=1.0, scalar=-3e38, op0=ALU.add, op1=ALU.max,
                        accum_out=row_max[:, 2 * h + t:2 * h + t + 1])
                    at += KEYS[t]
                ins.then_inc(*free(("s_c", h)))
                copied(dve, ("s_c", h))
                m = row_max[:, 2 * h:2 * h + 2]
                nc.vector.tensor_scalar(m, m, -MLA_SCALE, None, ALU.mult).then_inc(*masked.up())

            def divide(n):
                bank = filled(dve, ("o_c", n))
                part = den[:, 8 * n:8 * n + 8]
                lk(nc.vector.reciprocal(part, part))
                for t in range(TT):
                    ins = nc.vector.tensor_tensor(
                        tiles(O[t][:, 4 * n * HD:4 * (n + 1) * HD], HD), tiles(bank[:, t * T:(t + 1) * T], HD),
                        part[:, t::2].unsqueeze(2).to_broadcast([P, 4, HD]), ALU.mult)
                ins.then_inc(*o_ready.up())
                dve.wait_ge(o_ready.handle, n + 1)
                dve.sem_inc(*free(("o_c", n)))

            for i in range(H + 5):
                if i < H:
                    mask(i)
                if i >= 6 and i % 2 == 0:
                    m = (i - 6) // 2
                    dve.wait_ge(gate_sigmoid.handle, m + 1)
                    bank = filled(dve, ("rnn", m))
                    nc.vector.tensor_tensor(share[m], bank[:, 0:T], SGW[m % 4], ALU.mult).then_inc(*free(("rnn", m)))
                if i >= 5 and (i - 5) % 4 == 3:
                    dve.wait_ge(probs.handle, i - 4)
                    divide((i - 5) // 4)
            for quad in range(2):
                for t in range(TT):
                    key = ("turn", "o_c", t, quad)
                    bank = filled(dve, key)
                    nc.vector.tensor_copy(OT[:, 4 * quad:4 * quad + 4, t * P:(t + 1) * P], tiles(bank[:, :], P)).then_inc(*free(key))
            for m in range(KT):
                key = ("att", m)
                at = slice(m * T, (m + 1) * T)
                dve.wait_ge(gate_sigmoid.handle, KT + m + 1)
                bank = filled(dve, key)
                nc.vector.tensor_tensor(ST[:, at], bank[:, 0:T], SG[:, at], ALU.mult).then_inc(*free(key))
                copied(dve, key)
                nc.vector.tensor_tensor(Y[:, at], share[m], ST[:, at], ALU.add).then_inc(*mixed_ready.up())
            for m in range(KT):
                key = ("mix", m)
                bank = filled(dve, key)
                nc.vector.tensor_tensor(x[:, m, :], x[:, m, :], bank[:, 0:T], ALU.add).then_inc(*free(key))

        @block.sync
        def _(sp):
            sp.dma_start(RGW, g.names["rg_w"]).then_inc(*rgw_loaded.dma())
            core.load_weights(sp, g.stream, core.slot_no[("mix", KT - 1)] + 1 + RING)


def experts(nc, core, g):
    claim, full, filled, free, copied, link = core.claim, core.full, core.filled, core.free, core.copied, core.link
    cst, vec = cst_of(g), vec_of(g)
    taken = [0]

    def carve(width):
        taken[0] += width
        return core.arena[:, taken[0] - width:taken[0]]

    UNITS = [(h, t) for h in range(HP) for t in range(TT)]
    NU, NV, ND = 8, 6, 4
    x = tiles(g.res, S)[:, :, NM:]
    squares = carve(KT * T)
    n2 = tiles(carve(KT * T), T)
    X2, R = carve(TT * D), carve(TT * D)
    QT_ = tiles(carve(2 * HP * T), T)
    keys = carve(2 * NK)
    score = carve(len(UNITS) * 2 * NK)
    diag = [carve(P) for _ in range(ND)]
    U = [squares[:, n * D:(n + 1) * D] for n in range(TT)] + [carve(D) for _ in range(NU - TT)]
    V = [carve(D) for _ in range(NV)]
    w = [carve(TOPK * TOPK) for _ in range(5)]
    top, at_f = [carve(TOPK) for _ in range(2)], [carve(TOPK) for _ in range(2)]
    at_u, sel, digit = carve(2 * TOPK).bitcast(U32), carve(TOPK).bitcast(U32), carve(2 * TOPK)
    digit_u = carve(2 * TOPK).bitcast(U32)
    index_f, lead = carve(TOPK), carve(TOPK)
    chosen = carve(len(UNITS) * TOPK)
    index = carve(len(UNITS) * TOPK).bitcast(U32)
    weight, dots, act_out = (carve(len(UNITS) * TOPK) for _ in range(3))
    neg_max, total, dev = carve(len(UNITS)), carve(len(UNITS)), carve(2)
    rstd = g.wide[:, 0:T]
    final_g = g.rows[2]

    def sig(name):
        return core.counted("d_" + name)

    normed, keys_loaded, row_loaded = sig("normed"), sig("keys_loaded"), sig("row_loaded")
    routed, exped, weighed, dotted, activated, coef_ready = (
        sig(n) for n in ("routed", "exp", "weighed", "dotted", "activated", "coef"))
    u_used, v_used, diag_ready = sig("u_used"), sig("v_used"), sig("diag")
    u_landed, v_landed = [sig(f"u{n}_landed") for n in range(NU)], [sig(f"v{n}_landed") for n in range(NV)]
    summed, final_sq, final_dev, out_ready, stored = sig("summed"), sig("final_sq"), sig("final_dev"), sig("out"), sig("stored")

    def unit(ap, n):
        return ap[:, n * TOPK:(n + 1) * TOPK]

    def half(ap, t):
        return ap[:, t * D:(t + 1) * D]

    with nc.Block() as block:
        @block.tensor
        def _(pe):
            spare = [0]

            def take(key):
                spare[0] += 1
                return claim(pe, key, 4 + spare[0] % 4)

            pe.wait_ge(g.squared_d.handle, KT)
            bank = take("ss_d")
            for j in range(KT):
                mm = nc.tensor.matmul(bank[:, 0:T], cst("ones"), g.squares_d[:, j, :], start=j == 0, stop=j == KT - 1)
            mm.then_inc(*full("ss_d"))

            def route_inputs(h):
                for m in (2 * h, 2 * h + 1):
                    key = ("wq", m)
                    slot = core.weights(pe, key)
                    bank = take(key)
                    for k in range(KT):
                        if m == 0:
                            pe.wait_ge(normed.handle, k + 1)
                        mm = nc.tensor.matmul(bank[:, 0:T], slot[:, k * P:(k + 1) * P], n2[:, k, :], start=k == 0, stop=k == KT - 1)
                    mm.then_inc(*full(key))
                    core.used_by(key, key)
                for t in range(TT):
                    key = ("score", h, t)
                    bank = take(key)
                    for n in range(2):
                        copied(pe, ("wq", 2 * h + n))
                        mm = nc.tensor.matmul(bank[:, n * NK:(n + 1) * NK], QT_[:, 2 * h + n, t * P:(t + 1) * P],
                                              keys[:, n * NK:(n + 1) * NK], start=True, stop=True)
                    mm.then_inc(*full(key))

            def turn(name, src):
                for t in range(TT):
                    for quad in range(2):
                        key = ("turn", name, t, quad)
                        bank = take(key)
                        for i in range(4):
                            mm = nc.tensor.transpose(bank[:, i * P:(i + 1) * P], src[:, 4 * quad + i, t * P:(t + 1) * P], cst("ident"))
                        mm.then_inc(*full(key))

            pe.wait_ge(keys_loaded.handle, 16)
            route_inputs(0)
            turn("n2", n2)
            route_inputs(1)
            turn("x", x)
            route_inputs(2)
            for n, (h, t) in enumerate(UNITS):
                if t == 0 and h + 3 < HP:
                    route_inputs(h + 3)
                if h == 0:
                    for b in range(2):
                        claim(pe, ("sum", t, b), 2 * t + b)
                for k in range(TOPK):
                    i = n * TOPK + k
                    pe.wait_ge(v_landed[i % NV].handle, 16 * (i // NV + 1))
                    pe.wait_ge(diag_ready.handle, i + 1)
                    first, last = h == 0 and k == 0, h == HP - 1 and k == TOPK - 1
                    for b in range(2):
                        mm = nc.tensor.matmul(core.banks[2 * t + b][:, :], diag[i % ND], V[i % NV][:, b * 512:(b + 1) * 512],
                                              start=first, stop=last)
                    mm.then_inc(*v_used.up())

        @block.scalar
        def _(act):
            bank = filled(act, "ss_d")
            nc.scalar.activation(rstd, bank[:, 0:T], ACT.Sqrt, bias=g.eps[:, 0:1], scale=1.0 / D).then_inc(*free("ss_d"))

            def route_inputs(h):
                for m in (2 * h, 2 * h + 1):
                    bank = filled(act, ("wq", m))
                    nc.scalar.activation(QT_[:, m, :], bank[:, 0:T], ACT.Copy).then_inc(*free(("wq", m)))
                for t in range(TT):
                    n = 2 * h + t
                    bank = filled(act, ("score", h, t))
                    nc.scalar.activation(score[:, n * 2 * NK:(n + 1) * 2 * NK], bank[:, 0:2 * NK], ACT.Copy)\
                      .then_inc(*free(("score", h, t)))

            def turn(name, dst):
                for t in range(TT):
                    for quad in range(2):
                        key = ("turn", name, t, quad)
                        bank = filled(act, key)
                        nc.scalar.activation(dst[:, t * D + quad * 512:t * D + (quad + 1) * 512], bank[:, :], ACT.Copy)\
                          .then_inc(*free(key))

            def exps(n):
                act.wait_ge(routed.handle, n + 1)
                nc.scalar.activation(unit(weight, n), unit(chosen, n), ACT.Exp, bias=neg_max[:, n:n + 1],
                                     accum_out=total[:, n:n + 1]).then_inc(*exped.up())

            route_inputs(0)
            turn("n2", X2)
            exps(0)
            route_inputs(1)
            turn("x", R)
            exps(1)
            route_inputs(2)
            for n, (h, t) in enumerate(UNITS):
                act.wait_ge(dotted.handle, n + 1)
                nc.scalar.activation(unit(act_out, n), unit(dots, n), ACT.Gelu_apprx_tanh).then_inc(*activated.up())
                if t == 0 and h + 3 < HP:
                    route_inputs(h + 3)
                act.wait_ge(coef_ready.handle, n + 1)
                for k in range(TOPK):
                    i = n * TOPK + k
                    if i >= ND:
                        act.wait_ge(v_used.handle, i - ND + 1)
                    nc.scalar.activation(diag[i % ND], cst("ident"), ACT.Copy, scale=unit(act_out, n)[:, k:k + 1])\
                      .then_inc(*diag_ready.up())
                if n + 2 < len(UNITS):
                    exps(n + 2)
            for t in range(TT):
                act.wait_ge(summed.handle, t + 1)
                nc.scalar.activation(half(X2, t), half(R, t), ACT.Square, accum_out=dev[:, t:t + 1]).then_inc(*final_sq.up())
                act.wait_ge(final_sq.handle, t + 1)
                nc.scalar.activation(dev[:, t:t + 1], dev[:, t:t + 1], ACT.Sqrt, bias=g.eps[:, 0:1], scale=1.0 / D)\
                  .then_inc(*final_dev.up())

        @block.vector
        def _(dve):
            def lk(ins):
                link(dve, "dve", ins)

            copied(dve, "ss_d")
            lk(nc.vector.reciprocal(rstd, rstd))
            for j in range(KT):
                ins = nc.vector.scalar_tensor_tensor(out=n2[:, j, :], in0=x[:, j, :], scalar=vec("norm2", j), in1=rstd,
                                                     op0=ALU.mult, op1=ALU.mult)
                ins.then_inc(*normed.up())

            def top16(values, rest, best, where):
                lk(nc.vector.max(best[:, 0:8], values))
                nc.vector.max_index(where[:, 0:8], best[:, 0:8], values)
                lk(nc.vector.match_replace(rest, best[:, 0:8], values, -3e38))
                lk(nc.vector.max(best[:, 8:16], rest))
                lk(nc.vector.max_index(where[:, 8:16], best[:, 8:16], rest))

            def by_row(ap):
                return ap.unsqueeze(2).to_broadcast([P, TOPK, TOPK])

            def by_column(ap):
                return ap.unsqueeze(1).to_broadcast([P, TOPK, TOPK])

            def route(n):
                h, t = UNITS[n]
                copied(dve, ("score", h, t))
                for i in range(2):
                    at = (2 * n + i) * NK
                    top16(score[:, at:at + NK], w[i][:, 0:NK], top[i], at_u[:, i * TOPK:(i + 1) * TOPK])
                    lk(nc.vector.tensor_copy(at_f[i], at_u[:, i * TOPK:(i + 1) * TOPK]))
                lk(nc.vector.tensor_tensor(tiles(w[2], TOPK), by_row(top[0]), by_column(top[1]), ALU.add))
                top16(w[2], w[3], unit(chosen, n), sel)
                nc.vector.tensor_scalar(digit_u[:, 0:TOPK], sel, 4, None, ALU.logical_shift_right)
                lk(nc.vector.tensor_scalar(digit_u[:, TOPK:2 * TOPK], sel, 15, None, ALU.bitwise_and))
                lk(nc.vector.tensor_copy(digit, digit_u))
                nc.vector.tensor_scalar(neg_max[:, n:n + 1], unit(chosen, n)[:, 0:1], -1.0, None, ALU.mult)
                for i in range(2):
                    lk(nc.vector.tensor_tensor(tiles(w[i], TOPK), by_row(digit[:, i * TOPK:(i + 1) * TOPK]),
                                               by_column(cst("iota")), ALU.is_equal))
                    lk(nc.vector.tensor_tensor(tiles(w[i], TOPK), tiles(w[i], TOPK), by_column(at_f[i]), ALU.mult))
                    lk(nc.vector.tensor_reduce(lead if i == 0 else index_f, tiles(w[i], TOPK), AX.X, ALU.add))
                nc.vector.scalar_tensor_tensor(out=unit(index, n), in0=lead, scalar=float(NK), in1=index_f, op0=ALU.mult,
                                               op1=ALU.add).then_inc(*routed.up())
                dve.wait_ge(routed.handle, n + 1)

            def weigh(n):
                dve.wait_ge(exped.handle, n + 1)
                lk(nc.vector.reciprocal(total[:, n:n + 1], total[:, n:n + 1]))
                nc.vector.tensor_scalar(unit(weight, n), unit(weight, n), total[:, n:n + 1], None, ALU.mult).then_inc(*weighed.up())

            route(0)
            route(1)
            copied(dve, ("turn", "n2", 1, 1))
            for n, (h, t) in enumerate(UNITS):
                for k in range(TOPK):
                    i = n * TOPK + k
                    dve.wait_ge(u_landed[i % NU].handle, 16 * (i // NU + 1))
                    row = U[i % NU]
                    ins = nc.vector.tensor_tensor_reduce(out=row, in0=row, in1=half(X2, t), scale=1.0, scalar=0.0, op0=ALU.mult,
                                                         op1=ALU.add, accum_out=unit(dots, n)[:, k:k + 1])
                    ins.then_inc(*u_used.up())
                dve.wait_ge(u_used.handle, (n + 1) * TOPK)
                dve.sem_inc(*dotted.up())
                weigh(n)
                dve.wait_ge(activated.handle, n + 1)
                dve.wait_ge(weighed.handle, n + 1)
                nc.vector.tensor_tensor(unit(act_out, n), unit(act_out, n), unit(weight, n), ALU.mult).then_inc(*coef_ready.up())
                if n + 2 < len(UNITS):
                    route(n + 2)
            copied(dve, ("turn", "x", 1, 1))
            for t in range(TT):
                dve.wait_ge(v_used.handle, (len(UNITS) - TT + t + 1) * TOPK)
                for b in range(2):
                    at = half(R, t)[:, b * 512:(b + 1) * 512]
                    ins = nc.vector.tensor_tensor(at, at, core.banks[2 * t + b][:, :], ALU.add)
                ins.then_inc(*summed.up())
                dve.wait_ge(final_dev.handle, t + 1)
                dve.wait_ge(row_loaded.handle, 16)
                lk(nc.vector.reciprocal(dev[:, t:t + 1], dev[:, t:t + 1]))
                nc.vector.scalar_tensor_tensor(out=half(R, t), in0=half(R, t), scalar=dev[:, t:t + 1], in1=final_g, op0=ALU.mult,
                                               op1=ALU.mult).then_inc(*out_ready.up())

        @block.gpsimd
        def _(pool):
            def gather(table, rows, i, ring, landed, used):
                if i >= ring:
                    pool.wait_ge(used.handle, i - ring + 1)
                pool.indirect_dma_start(out=rows[i % ring], out_offset=None, in_=g.names[table],
                                        in_offset=bass.IndirectOffsetOnAxis(ap=index[:, i:i + 1], axis=0))\
                    .then_inc(*landed[i % ring].dma())

            pool.wait_ge(routed.handle, 1)
            for i in range(TOPK):
                gather("peer_u", U, i, NU, u_landed, u_used)
            for n in range(len(UNITS)):
                if n + 1 < len(UNITS):
                    pool.wait_ge(routed.handle, n + 2)
                for k in range(TOPK):
                    if n + 1 < len(UNITS):
                        gather("peer_u", U, (n + 1) * TOPK + k, NU, u_landed, u_used)
                    gather("peer_v", V, n * TOPK + k, NV, v_landed, v_used)

        @block.sync
        def _(sp):
            sp.dma_start(keys, g.names["keys"]).then_inc(*keys_loaded.dma())
            sp.dma_start(final_g, g.row(5)).then_inc(*row_loaded.dma())
            core.load_weights(sp, g.stream, len(core.slots))
            for t in range(TT):
                sp.wait_ge(out_ready.handle, t + 1)
                sp.dma_start(g.out[t * P:(t + 1) * P, :], half(R, t)).then_inc(*stored.dma())
            sp.wait_ge(stored.handle, 16 * TT)


class Globals:
    pass


def build(nc, names, out, stages=9):
    with ExitStack() as ctx:
        core = Core(nc, ctx)
        g = Globals()
        g.res = core.sbuf("res", KT * S)[:, :]
        g.cst = core.sbuf("cst", CONST_N)[:, :]
        g.vec = core.sbuf("vec", VEC_N)[:, :]
        g.rows = [core.sbuf(f"row{n}", D)[:, :] for n in range(3)]
        g.small = core.sbuf("small", 256)[:, :]
        g.wide = core.sbuf("wide", 1024)[:, :]
        g.eps = core.sbuf("eps", 4)[:, :]
        g.lora2 = core.arena[:, 12 * 2048:13 * 2048]
        g.res_in, g.cst_in, g.vec_in, g.low2_in = names["res"], names["cst"], names["vec"], names["low2"]
        g.stream = names["stream"]
        g.names = names
        g.out = out
        g.row = lambda n: names["rows"][n:n + 1, :].to_broadcast([P, D])
        g.ones_loaded, g.cst_loaded, g.vec_loaded, g.lora_loaded, g.rows_loaded, g.rows_reloaded, g.eps_set = (
            core.counted(n) for n in ("ones_loaded", "cst_loaded", "vec_loaded", "lora_loaded", "rows_loaded", "rows_reloaded", "eps_set"))
        g.x_loaded = [core.counted(f"x{n}_loaded") for n in range(2)]
        g.squares_c = tiles(core.arena[:, KT * S:2 * KT * S], S)
        g.squares_d = tiles(core.arena[:, 0:KT * T], T)
        g.squared_b, g.squared_c, g.squared_d = (core.counted(n) for n in ("squared_b", "squared_c", "squared_d"))
        for stage in (time_mix, moba, second_mix, experts)[:stages]:
            stage(nc, core, g)


def kernel(**inputs):
    import concourse.bacc as bacc
    from concourse.bass_utils import run_bass_kernel_spmd

    w = {k: np.asarray(v) for k, v in inputs.items()}
    res = np.concatenate([w["meta_tokens_2"], w["x"][0]], 0).T
    vectors = [w["norm_a"][0], w["mu_a"][0].reshape(-1), w["norm_kv"], w["norm_b"][0], np.tile(w["k_norm"], 2),
               np.tile(w["q_norm_b"][0], 2), w["norm1_g_2"][0], w["conv_w_2"][0].reshape(-1), w["conv_b_2"][0],
               w["rg_ba_2"][0], w["rg_bx_2"][0], w["rg_lambda_2"][0], w["q_norm_g_2"][0], w["kv_norm_g_2"][0],
               w["norm2_g_2"][0]]
    rows = [w["kk_a"][0], w["ka_a"][0], w["rk_a"][0].reshape(-1), w["gn_w_a"][0], w["gn_b_a"][0], w["final_g_2"]]
    low2 = [np.concatenate([w["w2_a"][0], w["w0_a"]], 0), np.concatenate([w["a2_a"][0], w["a0_a"]], 0)]
    arrays = {
        "res": res.reshape(KT, P, S).transpose(1, 0, 2).reshape(P, KT * S),
        "cst": constants(),
        "vec": np.concatenate([columns(v) for v in vectors], 1),
        "rows": np.stack(rows),
        "low2": np.concatenate(low2, 1),
        "stream": pack_weights(w),
        "rg_w": np.concatenate([w["rg_wa_2"][0].transpose(1, 0, 2).reshape(P, -1),
                                w["rg_wx_2"][0].transpose(1, 0, 2).reshape(P, -1)], 1),
        "keys": np.concatenate([w["peer_keys1_2"][0].T, w["peer_keys2_2"][0].T], 1),
        "peer_u": w["peer_u_2"][0],
        "peer_v": w["peer_v_2"][0],
    }
    arrays = {k: np.ascontiguousarray(v) for k, v in arrays.items()}
    nc = bacc.Bacc("TRN2", target_bir_lowering=False, num_devices=1)
    names = {k: nc.dram_tensor(k + "_in", a.shape, F32, kind="ExternalInput").ap() for k, a in arrays.items()}
    out = nc.dram_tensor("out", (T, D), F32, kind="ExternalOutput").ap()
    build(nc, names, out)
    r = run_bass_kernel_spmd(nc, [{k + "_in": a for k, a in arrays.items()}], core_ids=[0])
    return r.results[0]["out"].reshape(1, T, D)
```
